# Optimizing a Trainium2 kernel written in Bass

```python
import jax, jax.numpy as jnp
from jax import lax
import numpy as np

D_MODEL = 1024
BATCH = 1
SEQ = 256
DEPTH = 1
DEC_BATCH = 8
DEC_SEQ = 4
PAST_LEN = 2048
PAGE_SIZE = 128

D_CONV = D_MODEL // 2
CONV_WIDTH = 31
CONV_BUF = CONV_WIDTH - 1
D_POOL = D_MODEL // 2
POOL_WINDOWS = (2, 4, 8, 16)
N_POOL_GROUPS = len(POOL_WINDOWS)
POOL_GROUP_IN = D_POOL // N_POOL_GROUPS
POOL_GROUP_OUT = D_MODEL // N_POOL_GROUPS
POOL_BUF = max(POOL_WINDOWS) - 1
IN_COLS = 2 * D_CONV + D_POOL + 2 * D_MODEL
N_EXPERTS = 32
TOP_K = 4
D_EXPERT = D_MODEL
SWIGLU_LIMIT = 7.0
SWIGLU_ALPHA = 1.702
MOE_BLOCK = 128
N_MOD = 6
EPS = 1e-6

kernel_name = "gated_conv_pool_moe_decoder_step"

def rmsnorm(x, g):
    xf = x.astype(jnp.float32)
    y = xf * lax.rsqrt(jnp.mean(xf * xf, axis=-1, keepdims=True) + EPS)
    return (y * g.astype(jnp.float32)).astype(x.dtype)

def layernorm(x, g, b):
    xf = x.astype(jnp.float32)
    mu = jnp.mean(xf, axis=-1, keepdims=True)
    var = jnp.mean(jnp.square(xf - mu), axis=-1, keepdims=True)
    y = (xf - mu) * lax.rsqrt(var + EPS)
    return (y * g.astype(jnp.float32) + b.astype(jnp.float32)).astype(x.dtype)

def causal_depthwise_conv(u, buf, w, b):
    full = jnp.concatenate([buf.astype(u.dtype), u], axis=1)
    y = lax.conv_general_dilated(
        full, w[:, None, :].astype(u.dtype), window_strides=(1,), padding="VALID",
        dimension_numbers=("NWC", "WIO", "NWC"), feature_group_count=u.shape[-1])
    return y + b, full[:, -CONV_BUF:, :]

def causal_multiscale_pool(u, buf, pos0):
    T = u.shape[1]
    full = jnp.concatenate([buf.astype(u.dtype), u], axis=1)
    fullf = full.astype(jnp.float32)
    cs = jnp.pad(jnp.cumsum(fullf, axis=1), ((0, 0), (1, 0), (0, 0)))
    pos = pos0 + jnp.arange(T, dtype=jnp.int32)
    outs = []
    for g, win in enumerate(POOL_WINDOWS):
        lo, hi = g * POOL_GROUP_IN, (g + 1) * POOL_GROUP_IN
        end = cs[:, POOL_BUF + 1:POOL_BUF + 1 + T, lo:hi]
        start = cs[:, POOL_BUF + 1 - win:POOL_BUF + 1 - win + T, lo:hi]
        cnt = jnp.minimum(pos + 1, win).astype(jnp.float32)[None, :, None]
        outs.append((end - start) / cnt - fullf[:, POOL_BUF:, lo:hi])
    pooled = jnp.stack(outs, axis=2).astype(u.dtype)
    return pooled, full[:, -POOL_BUF:, :]

def token_mixer(h, conv_buf, pool_buf, pos0, w_in, b_in, conv_w, conv_b, ln_g, ln_b,
                w_conv_out, w_pool, pool_scale, w_out):
    B, T, _ = h.shape
    z = h @ w_in + b_in
    u_val, u_gate, u_pool, g_conv, g_pool = jnp.split(
        z, [D_CONV, 2 * D_CONV, 2 * D_CONV + D_POOL, 2 * D_CONV + D_POOL + D_MODEL], axis=-1)
    u = u_val * jax.nn.sigmoid(u_gate)
    v, new_conv_buf = causal_depthwise_conv(u, conv_buf, conv_w, conv_b)
    v = jax.nn.silu(layernorm(v, ln_g, ln_b))
    y_conv = v @ w_conv_out
    pooled, new_pool_buf = causal_multiscale_pool(u_pool, pool_buf, pos0)
    y_pool = jnp.einsum("btgi,gio->btgo", pooled, w_pool).reshape(B, T, D_MODEL) * pool_scale
    m = jax.nn.sigmoid(g_conv) * y_conv + jax.nn.sigmoid(g_pool) * y_pool
    return m @ w_out, new_conv_buf, new_pool_buf

def routed_experts(h, w_router, b_router, w_up, b_up, w_down, b_down):
    B, T, D = h.shape
    n_tok = B * T
    x = h.reshape(n_tok, D)
    logits = (x @ w_router + b_router).astype(jnp.float32)
    top_logit, top_idx = lax.top_k(logits, TOP_K)
    top_w = jax.nn.softmax(top_logit, axis=-1)
    n_assign = n_tok * TOP_K
    n_blocks = n_assign // MOE_BLOCK + N_EXPERTS + 1
    n_slots = n_blocks * MOE_BLOCK
    flat_e = top_idx.reshape(n_assign)
    flat_tok = jnp.arange(n_assign, dtype=jnp.int32) // TOP_K
    flat_w = top_w.reshape(n_assign)
    order = jnp.argsort(flat_e)
    e_sorted = flat_e[order]
    counts = jnp.bincount(flat_e, length=N_EXPERTS)
    padded = (counts + MOE_BLOCK - 1) // MOE_BLOCK * MOE_BLOCK
    pad_end = jnp.cumsum(padded)
    pad_start = pad_end - padded
    raw_start = jnp.cumsum(counts) - counts
    dest = pad_start[e_sorted] + jnp.arange(n_assign, dtype=jnp.int32) - raw_start[e_sorted]
    slot_tok = jnp.full((n_slots,), n_tok, jnp.int32).at[dest].set(flat_tok[order])
    slot_w = jnp.zeros((n_slots,), jnp.float32).at[dest].set(flat_w[order])
    block_expert = jnp.minimum(
        jnp.searchsorted(pad_end, jnp.arange(n_blocks, dtype=jnp.int32) * MOE_BLOCK, side="right"),
        N_EXPERTS - 1)
    x_pad = jnp.concatenate([x, jnp.zeros((1, D), x.dtype)], axis=0)
    xb = x_pad[slot_tok].reshape(n_blocks, MOE_BLOCK, D)

    def expert_block(args):
        xk, e = args
        a = xk @ w_up[e] + b_up[e]
        a_glu = jnp.minimum(a[:, :D_EXPERT], SWIGLU_LIMIT)
        a_lin = jnp.clip(a[:, D_EXPERT:], -SWIGLU_LIMIT, SWIGLU_LIMIT)
        o = a_glu * jax.nn.sigmoid(SWIGLU_ALPHA * a_glu) * (a_lin + 1)
        return o @ w_down[e] + b_down[e]

    yb = lax.map(expert_block, (xb, block_expert))
    y = yb.reshape(n_slots, D).astype(jnp.float32) * slot_w[:, None]
    out = jax.ops.segment_sum(y, slot_tok, num_segments=n_tok + 1)[:n_tok]
    return out.astype(h.dtype).reshape(B, T, D)

def trunk(x, c, conv_bufs, pool_bufs, pos0, w_ada, b_ada, norm_mix, w_in, b_in, conv_w, conv_b,
          conv_ln_g, conv_ln_b, w_conv_out, w_pool, pool_scale, w_out, norm_ffn, w_router,
          b_router, w_up, b_up, w_down, b_down, norm_final):
    new_conv, new_pool = [], []
    for l in range(DEPTH):
        mod = (jax.nn.silu(c) @ w_ada[l] + b_ada[l])[:, None, :]
        sh1, sc1, gt1, sh2, sc2, gt2 = jnp.split(mod, N_MOD, axis=-1)
        h = rmsnorm(x, norm_mix[l]) * (1 + sc1) + sh1
        y, cb, pb = token_mixer(h, conv_bufs[l], pool_bufs[l], pos0, w_in[l], b_in[l], conv_w[l],
                                conv_b[l], conv_ln_g[l], conv_ln_b[l], w_conv_out[l], w_pool[l],
                                pool_scale[l], w_out[l])
        x = x + gt1 * y
        h = rmsnorm(x, norm_ffn[l]) * (1 + sc2) + sh2
        x = x + gt2 * routed_experts(h, w_router[l], b_router[l], w_up[l], b_up[l], w_down[l], b_down[l])
        new_conv.append(cb)
        new_pool.append(pb)
    return rmsnorm(x, norm_final), jnp.stack(new_conv), jnp.stack(new_pool)

def setup_inputs(seed: int = 0) -> dict:
    key = jax.random.key(seed)
    ks = jax.random.split(key, 32)
    f32 = jnp.float32
    nrm = lambda k, shape, s: jax.random.normal(k, shape, f32) * s
    D = D_MODEL
    return {
        "x_prompt": nrm(ks[0], (BATCH, SEQ, D), 1.0),
        "x_sample": nrm(ks[1], (DEC_BATCH, DEC_SEQ, D), 1.0),
        "state_conv": nrm(ks[2], (DEPTH, DEC_BATCH, CONV_BUF, D_CONV), 0.5),
        "state_pool": nrm(ks[3], (DEPTH, DEC_BATCH, POOL_BUF, D_POOL), 1.0),
        "c_prompt": nrm(ks[4], (BATCH, D), 1.0),
        "c_sample": nrm(ks[5], (DEC_BATCH, D), 1.0),
        "w_ada": nrm(ks[6], (DEPTH, D, N_MOD * D), 0.5 * D ** -0.5),
        "b_ada": nrm(ks[7], (DEPTH, N_MOD * D), 0.02),
        "norm_mix": 1.0 + nrm(ks[8], (DEPTH, D), 0.05),
        "w_in": nrm(ks[9], (DEPTH, D, IN_COLS), D ** -0.5),
        "b_in": nrm(ks[10], (DEPTH, IN_COLS), 0.02),
        "conv_w": nrm(ks[11], (DEPTH, CONV_WIDTH, D_CONV), CONV_WIDTH ** -0.5),
        "conv_b": nrm(ks[12], (DEPTH, D_CONV), 0.02),
        "conv_ln_g": 1.0 + nrm(ks[13], (DEPTH, D_CONV), 0.05),
        "conv_ln_b": nrm(ks[14], (DEPTH, D_CONV), 0.02),
        "w_conv_out": nrm(ks[15], (DEPTH, D_CONV, D), D_CONV ** -0.5),
        "w_pool": nrm(ks[16], (DEPTH, N_POOL_GROUPS, POOL_GROUP_IN, POOL_GROUP_OUT), POOL_GROUP_IN ** -0.5),
        "pool_scale": 1.0 + nrm(ks[17], (DEPTH, D), 0.1),
        "w_out": nrm(ks[18], (DEPTH, D, D), D ** -0.5),
        "norm_ffn": 1.0 + nrm(ks[19], (DEPTH, D), 0.05),
        "w_router": nrm(ks[20], (DEPTH, D, N_EXPERTS), D ** -0.5),
        "b_router": nrm(ks[21], (DEPTH, N_EXPERTS), 0.01),
        "w_up": nrm(ks[22], (DEPTH, N_EXPERTS, D, 2 * D_EXPERT), D ** -0.5),
        "b_up": nrm(ks[23], (DEPTH, N_EXPERTS, 2 * D_EXPERT), 0.02),
        "w_down": nrm(ks[24], (DEPTH, N_EXPERTS, D_EXPERT, D), D_EXPERT ** -0.5),
        "b_down": nrm(ks[25], (DEPTH, N_EXPERTS, D), 0.02),
        "norm_final": 1.0 + nrm(ks[26], (D,), 0.05),
    }

def reference(x_prompt, x_sample, state_conv, state_pool, c_prompt, c_sample, w_ada, b_ada,
              norm_mix, w_in, b_in, conv_w, conv_b, conv_ln_g, conv_ln_b, w_conv_out, w_pool,
              pool_scale, w_out, norm_ffn, w_router, b_router, w_up, b_up, w_down, b_down,
              norm_final):
    weights = (w_ada, b_ada, norm_mix, w_in, b_in, conv_w, conv_b, conv_ln_g, conv_ln_b,
               w_conv_out, w_pool, pool_scale, w_out, norm_ffn, w_router, b_router, w_up, b_up,
               w_down, b_down, norm_final)
    B = x_prompt.shape[0]
    zero_conv = jnp.zeros((DEPTH, B, CONV_BUF, D_CONV), x_prompt.dtype)
    zero_pool = jnp.zeros((DEPTH, B, POOL_BUF, D_POOL), x_prompt.dtype)
    y_prompt, new_conv_prompt, new_pool_prompt = trunk(
        x_prompt, c_prompt, zero_conv, zero_pool, 0, *weights)
    y_sample, new_conv_sample, new_pool_sample = trunk(
        x_sample, c_sample, state_conv, state_pool, PAST_LEN, *weights)
    return (y_prompt, y_sample, new_conv_prompt, new_pool_prompt, new_conv_sample, new_pool_sample)


_drawn_inputs = setup_inputs


def setup_inputs(seed=0):
    import zlib

    import numpy as np

    out = dict(_drawn_inputs(seed))
    spreads = {}
    factors = {'b_in': 2.886,
     'conv_b': 5.084,
     'conv_ln_g': 6.036,
     'conv_ln_b': 25.654,
     'b_router': 18.731,
     'b_up': 8.0,
     'b_down': 22.66,
     'pool_scale': 3.464}
    for name, (base, spread) in spreads.items():
        noise = np.random.default_rng([zlib.crc32(name.encode()), seed]).standard_normal(out[name].shape)
        drawn = base * np.exp(spread * noise) if base else spread * noise
        out[name] = __import__('jax').numpy.asarray(drawn.astype(out[name].dtype))
    for name, factor in factors.items():
        out[name] = (out[name] * factor).astype(out[name].dtype)
    return out
```

```python
from contextlib import ExitStack

import concourse.bass as bass
from concourse import mybir

P = 128
F32 = mybir.dt.float32
I32 = mybir.dt.int32
ALU = mybir.AluOpType
ACT = mybir.ActivationFunctionType
AX = mybir.AxisListType

D = 1024
KT = D // P
SEQ = 256
DEC_B, DEC_T = 8, 4
DEC = DEC_B * DEC_T
NT = SEQ + DEC
SEQS = 1 + DEC_B
TOK_TILES = [(0, P), (P, P), (2 * P, NT - 2 * P)]
NJ = len(TOK_TILES)
DC = D // 2
CT_ = DC // P
TAPS = 31
CBUF = TAPS - 1
WINDOWS = (2, 4, 8, 16)
PBUF = max(WINDOWS) - 1
NE = 32
TOPK = 4
LIMIT = 7.0
ALPHA = 1.702
EPS = 1e-6

SLOTS = 128
WIDTHS = (64, 96)
PASSES = (NT + SLOTS - 1) // SLOTS

RING = 6
COLS = 512
BANK = 512

MIXER_CHUNKS = ([("ada", i) for i in range(4)] + [("in", i) for i in range(7)] +
                [("ada", 4), ("ada", 5), ("conv_out", 0), ("ada", 6), ("ada", 7),
                 ("out", 0), ("out", 1)] + [("ada", i) for i in range(8, 12)])
NMIX = len(MIXER_CHUNKS)
MIX_AT = {c: i for i, c in enumerate(MIXER_CHUNKS)}
EXPERT_CHUNKS = 6

VEC_ROWS = {}
_at = 0
for _name, _n in (("b_ada", 48), ("b_in", 28), ("norm_mix", 8), ("norm_ffn", 8), ("norm_final", 8),
                  ("pool_scale", 8), ("conv_b", 4), ("conv_ln_g", 4), ("conv_ln_b", 4)):
    VEC_ROWS[_name] = (_at, _n)
    _at += _n
NVEC = _at

PF_W = (PBUF + SEQ) + DEC_B * (PBUF + DEC_T)
UF_W = (CBUF + SEQ) + DEC_B * (CBUF + DEC_T)


def build(nc, x_prompt, x_sample, state_conv, state_pool, c_prompt, c_sample, w_ada, b_ada, norm_mix,
          w_in, b_in, conv_w, conv_b, conv_ln_g, conv_ln_b, w_conv_out, w_pool, pool_scale, w_out,
          norm_ffn, w_router, b_router, w_up, b_up, w_down, b_down, norm_final,
          y_prompt, y_sample, new_conv_prompt, new_pool_prompt, new_conv_sample, new_pool_sample):
    with ExitStack() as ctx:
        def sb(name, shape, dt=F32):
            return ctx.enter_context(nc.sbuf_tensor(name, shape, dt))

        def sem(name):
            return ctx.enter_context(nc.semaphore(name))

        ring = sb("ring", [P, RING, KT * COLS])
        vec = sb("vec", [P, P])
        taps = sb("taps", [P, CT_, TAPS])
        rows = sb("rows", [P, NJ, D])
        wrouter = sb("wrouter", [P, KT, NE])
        wpool = sb("wpool", [P, CT_, 2 * P])
        xT = sb("xT", [P, KT, NT])
        hT = sb("hT", [P, KT, NT])
        sq = sb("sq", [P, KT, NT])
        uv = sb("uv", [P, KT, NT])
        sg = sb("sg", [P, 2 * KT * NT])
        ufull = sb("ufull", [P, CT_ * UF_W])
        pf = sb("pf", [P, CT_ * PF_W])
        pa = sb("pa", [P, CT_ * PF_W])
        pb = sb("pb", [P, CT_ * PF_W])
        modT = sb("modT", [P, 6 * KT, SEQS])
        silc = sb("silc", [P, KT, SEQS])
        bupT = sb("bupT", [P, 2 * KT, NE])
        ident = sb("ident", [P, P])
        upper = sb("upper", [P, P])
        ones = sb("ones", [P, P])
        avg = sb("avg", [P, 2, P])
        epsc = sb("epsc", [P, 1])
        rms = sb("rms", [P, NT])
        rstd = sb("rstd", [P, NT])
        iota = sb("iota", [P, SLOTS])
        icnt = sb("icnt", [P, CT_, 16])
        brout = sb("brout", [P, NE])
        top8 = sb("top8", [P, NJ, 8])
        need = sb("need", [P, NJ])
        wgt = sb("wgt", [P, NJ, NE])
        rankm = sb("rankm", [P, NJ, NE + 1])
        cntf = sb("cntf", [1, NE + 2])
        cnti = sb("cnti", [1, NE + 2], I32)

        tap_rows = pa[0:TAPS, 0:DC]
        vec_rows = pb[:, 0:P]
        bdown = wpool[0:NE, :, :].rearrange("p g n -> p (g n)")
        wT = pa[0:NE, 0:NT]
        lg, mask, eq, cum = (ufull[:, a:a + NJ * NE].rearrange("p (j e) -> p j e", e=NE)
                             for a in range(2 * NJ * SLOTS + NT, 2 * NJ * SLOTS + NT + 4 * NJ * NE, NJ * NE))

        bup_rows = sg[0:NE, 0:2 * D]
        sconv_rows = sg[0:120, 2 * D:2 * D + 2 * DC].rearrange("p (j d) -> p j d", j=2)
        c_rows = sg[0:SEQS, 3 * D:4 * D]
        spool_rows = sg[0:120, 4 * D:4 * D + DC]
        sgT = sg[:, :].rearrange("p (t n) -> p t n", n=NT)
        hgT = sg[:, 0:KT * SLOTS].rearrange("p (k s) -> p k s", s=SLOTS)
        oT = sg[:, KT * SLOTS:2 * KT * SLOTS].rearrange("p (k s) -> p k s", s=SLOTS)
        ysT = sg[:, 2 * KT * SLOTS:3 * KT * SLOTS].rearrange("p (k s) -> p k s", s=SLOTS)
        yrow = sg[:, 3 * KT * SLOTS:4 * KT * SLOTS]
        hot = ufull[:, 0:NJ * SLOTS].rearrange("p (j s) -> p j s", s=SLOTS)
        hotw = ufull[:, NJ * SLOTS:2 * NJ * SLOTS].rearrange("p (j s) -> p j s", s=SLOTS)
        comb = ufull[:, 2 * NJ * SLOTS:2 * NJ * SLOTS + NT]
        glu = pf[:, 0:2 * BANK].rearrange("p (h n) -> p h n", h=2)
        sig = pa[:, 0:2 * BANK].rearrange("p (h n) -> p h n", h=2)
        lin = pb[:, 0:2 * BANK].rearrange("p (h n) -> p h n", h=2)
        uf = ufull[:, :].rearrange("p (c n) -> p c n", c=CT_)
        uf_p = uf[:, :, 0:CBUF + SEQ]
        uf_s = uf[:, :, CBUF + SEQ:UF_W].rearrange("p c (s t) -> p c s t", s=DEC_B)
        pool_bufs = []
        for buf in (pf, pa, pb):
            v = buf[:, :].rearrange("p (c n) -> p c n", c=CT_)
            pool_bufs.append((v[:, :, 0:PBUF + SEQ],
                              v[:, :, PBUF + SEQ:PF_W].rearrange("p c (s t) -> p c s t", s=DEC_B)))
        uT = uv[:, 0:CT_, :]
        vT = uv[:, CT_:KT, :]
        accT = uv
        gateT = sq[:, 0:CT_, :]
        upT = sq[:, CT_:KT, :]
        stage = rows[:, :, :].rearrange("p j d -> p (j d)")

        def vcol(name, i):
            return vec[:, VEC_ROWS[name][0] + i:VEC_ROWS[name][0] + i + 1]

        def vcols(name):
            a, n = VEC_ROWS[name]
            return vec[:, a:a + n]

        def decoded(ap):
            return ap[:, :, SEQ:NT].rearrange("p k (s t) -> p k s t", t=DEC_T)

        ps = ctx.enter_context(nc.psum_tensor("ps", [P, 8, BANK], F32))

        ld_vec = sem("ld_vec")
        ld_x = sem("ld_x")
        ld_c = sem("ld_c")
        ld_taps = sem("ld_taps")
        ld_state = sem("ld_state")
        ld_bup = sem("ld_bup")
        ld_late = sem("ld_late")
        ld_bdown = sem("ld_bdown")
        landed = [sem(f"landed{i}") for i in range(RING)]
        chunk_used = sem("chunk_used")
        consts = sem("consts")
        zeroed = sem("zeroed")
        silu_c = sem("silu_c")
        turned = sem("turned")
        turn_out = sem("turn_out")
        sq1 = sem("sq1")
        stat1 = sem("stat1")
        rms1 = sem("rms1")
        h1 = sem("h1")
        z_done = sem("z_done")
        z_out = sem("z_out")
        u_ready = sem("u_ready")
        uf_ready = sem("uf_ready")
        vs_conv = sem("vs_conv")
        v_ready = sem("v_ready")
        st_turned = sem("st_turned")
        st_out = sem("st_out")
        pool_step = sem("pool_step")
        pooled = sem("pooled")
        mean_done = sem("mean_done")
        centred = sem("centred")
        vsq = sem("vsq")
        var_done = sem("var_done")
        vrms = sem("vrms")
        ln_ready = sem("ln_ready")
        ln_sig = sem("ln_sig")
        vact = sem("vact")
        yp_done = sem("yp_done")
        yp_out = sem("yp_out")
        yc_done = sem("yc_done")
        m_ready = sem("m_ready")
        yo_done = sem("yo_done")
        x2_out = sem("x2_out")
        sq2 = sem("sq2")
        stat2 = sem("stat2")
        rms2 = sem("rms2")
        h2 = sem("h2")
        logits = sem("logits")
        h2_turned = sem("h2_turned")
        h2_out = sem("h2_out")
        shifted = sem("shifted")
        expd = sem("expd")
        mask_ready = sem("mask_ready")
        wgt_ready = sem("wgt_ready")
        ranked = sem("ranked")
        rank_ready = sem("rank_ready")
        wT_turned = sem("wT_turned")
        wT_out = sem("wT_out")
        bd_done = sem("bd_done")
        bd_out = sem("bd_out")
        hg_clear = sem("hg_clear")
        pass_ready = sem("pass_ready")
        hot_ready = sem("hot_ready")
        hotw_ready = sem("hotw_ready")
        gathered = sem("gathered")
        hg_out = sem("hg_out")
        glu_out = sem("glu_out")
        lin_out = sem("lin_out")
        sig_out = sem("sig_out")
        lin_clip = sem("lin_clip")
        gs_out = sem("gs_out")
        o_ready = sem("o_ready")
        y_out = sem("y_out")
        y_turned = sem("y_turned")
        yrow_out = sem("yrow_out")
        combined = sem("combined")
        added = sem("added")
        comb_turned = sem("comb_turned")
        comb_out = sem("comb_out")
        x3_out = sem("x3_out")
        sq3 = sem("sq3")
        stat3 = sem("stat3")
        rms3 = sem("rms3")
        yn = sem("yn")
        fin_turned = sem("fin_turned")
        fin_out = sem("fin_out")
        st_sent = sem("st_sent")
        old_sent = sem("old_sent")
        y_sent = sem("y_sent")
        dve_done = sem("dve_done")
        pool_done = sem("pool_done")

        UP_BANKS = (0, 1, 2, 0, 1, 2)
        HG_BANK = 3
        T_BANK = 5
        BD_BANKS = (0, 1, 2, 7)
        GAT = NE + 1

        block = ctx.enter_context(nc.Block())

        @block.sync
        def _(sp):
            def source(kind, i):
                cols = slice(i * COLS, (i + 1) * COLS)
                if kind == "conv_out":
                    return w_conv_out[0].rearrange("(k p) n -> p k n", p=P)
                w = {"ada": w_ada, "in": w_in, "out": w_out}[kind]
                return w[0].rearrange("(k p) n -> p k n", p=P)[:, :, cols]

            for c, (kind, i) in enumerate(MIXER_CHUNKS):
                if c >= RING:
                    sp.wait_ge(chunk_used, c - RING + 1)
                src = source(kind, i)
                dst = ring[:, c % RING, :].rearrange("p (k n) -> p k n", k=src.shape[1])
                sp.dma_start(dst, src).then_inc(landed[c % RING], 16)

            up = w_up[0].rearrange("e (k p) n -> e p k n", p=P)
            down = w_down[0].rearrange("e (k p) n -> e p k n", p=P)

            def expert_weights(n, e):
                for j, (w, col) in enumerate(((up, 0), (up, D), (up, COLS), (up, D + COLS),
                                              (down, 0), (down, COLS))):
                    c = NMIX + j
                    sp.wait_ge(chunk_used, n * EXPERT_CHUNKS + (c - RING + 1))
                    dst = ring[:, c % RING, :].rearrange("p (k n) -> p k n", k=KT)
                    sp.dma_start(dst, w[e, :, :, col:col + COLS]).then_inc(landed[c % RING], 16)

            with sp.Fori(0, NE) as e:
                expert_weights(e, e)
            sp.wait_ge(rank_ready, 1)
            most = sp.value_load(cnti[0:1, NE + 1:NE + 2], min_val=0, max_val=NT)
            with sp.If(most > SLOTS):
                with sp.Fori(1, PASSES) as p:
                    with sp.Fori(0, NE) as e:
                        expert_weights(p * NE + e, e)

            sp.wait_ge(fin_out, 2)
            sp.dma_start(y_prompt[0, 0:P, :], rows[:, 0, :]).then_inc(y_sent, 16)
            sp.wait_ge(fin_out, 4)
            sp.dma_start(y_prompt[0, P:2 * P, :], rows[:, 1, :]).then_inc(y_sent, 16)
            sp.wait_ge(fin_out, 6)
            sp.dma_start(y_sample.rearrange("b t d -> (b t) d"), rows[0:DEC, 2, :]).then_inc(y_sent, 16)
            sp.wait_ge(y_sent, 3 * 16)
            sp.wait_ge(st_sent, 16 * (2 + 2 * DEC_B))

        @block.gpsimd
        def _(pool):
            pool.memset(ident[:, :], 0.0).then_inc(zeroed, 1)
            pool.memset(upper[:, :], 0.0).then_inc(zeroed, 1)
            pool.memset(ones[:, :], 1.0).then_inc(consts, 1)
            pool.memset(avg[:, 0, :], 1.0 / D).then_inc(consts, 1)
            pool.memset(avg[:, 1, :], 1.0 / DC).then_inc(consts, 1)
            pool.memset(epsc[:, :], EPS).then_inc(consts, 1)
            pool.wait_ge(zeroed, 2)
            pool.affine_select(out=ident[:, :], in_=ident[:, :], compare_op=ALU.not_equal, fill=1.0,
                               base=0, pattern=[[-1, P]], channel_multiplier=1).then_inc(consts, 1)
            pool.affine_select(out=upper[:, :], in_=upper[:, :], compare_op=ALU.is_ge, fill=1.0,
                               base=0, pattern=[[-1, P]], channel_multiplier=1).then_inc(consts, 1)
            pool.dma_start(new_conv_sample[0, :, 0:CBUF - DEC_T, :],
                           state_conv[0, :, DEC_T:CBUF, :]).then_inc(old_sent, 16)
            pool.dma_start(new_pool_sample[0, :, 0:PBUF - DEC_T, :],
                           state_pool[0, :, DEC_T:PBUF, :]).then_inc(old_sent, 16)
            pool.iota(iota[:, :], pattern=[[1, SLOTS]], base=0, channel_multiplier=0,
                      allow_small_or_imprecise_dtypes=True).then_inc(consts, 1)
            pool.iota(icnt[:, :, :], pattern=[[0, CT_], [1, 16]], base=1, channel_multiplier=0,
                      allow_small_or_imprecise_dtypes=True).then_inc(pool_done, 1)
            pool.wait_ge(pool_done, 1)
            for g, w in enumerate(WINDOWS):
                pool.tensor_scalar(icnt[:, g, :], icnt[:, g, :], float(w), None, ALU.min)\
                    .then_inc(consts, 1)
            (f_p, f_s), (a_p, a_s), (b_p, b_s) = pool_bufs
            pool.memset(f_p[:, :, 0:PBUF], 0.0).then_inc(pool_step, 1)
            pool.wait_ge(z_out, 3 * CT_)
            pool.wait_ge(turn_out, 16)
            pool.tensor_copy(f_p[:, :, PBUF:PBUF + SEQ], upT[:, :, 0:SEQ]).then_inc(pool_step, 1)
            for g in range(CT_):
                pool.tensor_copy(f_s[:, g, :, PBUF:PBUF + DEC_T],
                                 upT[:, g, SEQ:NT].rearrange("p (s t) -> p s t", t=DEC_T))\
                    .then_inc(pool_step, 1)
            pool.wait_ge(pool_step, 2 + CT_)
            src, dst = (f_p, f_s), (a_p, a_s)
            for g, w in enumerate(WINDOWS):
                lag, first = w // 2, w - 1
                pool.tensor_tensor(dst[0][:, g:, first:], src[0][:, g:, first:],
                                   src[0][:, g:, first - lag:PBUF + SEQ - lag], ALU.add)\
                    .then_inc(pool_step, 1)
                for q in range(g, CT_):
                    pool.tensor_tensor(dst[1][:, q, :, first:], src[1][:, q, :, first:],
                                       src[1][:, q, :, first - lag:PBUF + DEC_T - lag], ALU.add)\
                        .then_inc(pool_step, 1)
                pool.wait_ge(pool_step, 2 + CT_ + (g + 1) + sum(CT_ - q for q in range(g + 1)))
                src, dst = dst, ((b_p, b_s) if g % 2 == 0 else (a_p, a_s))

            pool.wait_ge(old_sent, 32)
            pool.wait_ge(yp_done, KT)
            pool.dma_start(bdown, b_down[0]).then_inc(ld_bdown, 16)

        @block.scalar
        def _(act):
            act.dma_start(rows[:, 0:2, :], x_prompt[0].rearrange("(j p) d -> p j d", p=P)).then_inc(ld_x, 16)
            act.dma_start(rows[0:DEC, 2, :], x_sample.rearrange("b t d -> (b t) d")).then_inc(ld_x, 16)
            act.dma_start(c_rows[0:1, :], c_prompt).then_inc(ld_c, 16)
            act.dma_start(c_rows[1:SEQS, :], c_sample).then_inc(ld_c, 16)
            for name, ap in (("b_ada", b_ada[0]), ("b_in", b_in[0]), ("norm_mix", norm_mix[0]),
                             ("norm_ffn", norm_ffn[0]), ("norm_final", norm_final),
                             ("pool_scale", pool_scale[0]), ("conv_b", conv_b[0]),
                             ("conv_ln_g", conv_ln_g[0]), ("conv_ln_b", conv_ln_b[0])):
                a, n = VEC_ROWS[name]
                act.dma_start(vec_rows[a:a + n, :], ap.rearrange("(r p) -> r p", p=P)).then_inc(ld_vec, 16)
            act.dma_start(tap_rows[:, :], conv_w[0]).then_inc(ld_taps, 16)
            act.dma_start(sconv_rows, state_conv[0].rearrange("s t d -> (s t) d")
                          .rearrange("(j p) d -> p j d", j=2)).then_inc(ld_state, 16)
            act.dma_start(spool_rows, state_pool[0].rearrange("s t d -> (s t) d")).then_inc(ld_state, 16)
            act.dma_start(bup_rows, b_up[0]).then_inc(ld_bup, 16)
            act.dma_start(wpool[:, :, :], w_pool[0].rearrange("g p n -> p g n")).then_inc(ld_late, 16)
            act.dma_start(wrouter[:, :, :], w_router[0].rearrange("(k p) n -> p k n", p=P)).then_inc(ld_late, 16)
            act.dma_start(brout[:, :], b_router.broadcast_to([P, NE])).then_inc(ld_late, 16)

            act.wait_ge(ld_c, 32)
            act.activation(sq[0:SEQS, 0:4, 0:256], c_rows.rearrange("p (k n) -> p k n", k=4),
                           ACT.Sigmoid).then_inc(silu_c, 1)

            for k in range(KT):
                act.wait_ge(turn_out, k + 2)
                if k == 0:
                    act.wait_ge(silu_c, 2)
                act.activation(sq[:, k, :], xT[:, k, :], ACT.Square).then_inc(sq1, 1)
            act.wait_ge(stat1, 1)
            act.wait_ge(consts, 4)
            act.activation(rms[:, :], ps[:, 1, 0:NT], ACT.Sqrt, bias=epsc[:, :]).then_inc(rms1, 1)

            for t in range(28):
                act.wait_ge(z_done, t + 1)
                src, bias = ps[:, t % 8, 0:NT], vcol("b_in", t)
                if t < CT_:
                    act.activation(uT[:, t, :], src, ACT.Identity, bias=bias).then_inc(z_out, 1)
                elif t < 2 * CT_:
                    act.activation(gateT[:, t - CT_, :], src, ACT.Sigmoid, bias=bias).then_inc(z_out, 1)
                elif t < 3 * CT_:
                    act.activation(upT[:, t - 2 * CT_, :], src, ACT.Identity, bias=bias).then_inc(z_out, 1)
                else:
                    act.activation(sgT[:, t - 3 * CT_, :], src, ACT.Sigmoid, bias=bias).then_inc(z_out, 1)

            for i in range(4):
                n = (CBUF, DEC, PBUF, DEC)[i]
                act.wait_ge(st_turned, i + 1)
                act.copy(stage[0:n, i * DC:(i + 1) * DC], ps[0:n, i, :]).then_inc(st_out, 1)
            act.wait_ge(st_out, 4)
            act.dma_start(new_conv_prompt[0, 0], stage[0:CBUF, 0:DC]).then_inc(st_sent, 16)
            act.dma_start(new_pool_prompt[0, 0], stage[0:PBUF, 2 * DC:3 * DC]).then_inc(st_sent, 16)
            for s in range(DEC_B):
                act.dma_start(new_conv_sample[0, s, CBUF - DEC_T:CBUF, :],
                              stage[s * DEC_T:(s + 1) * DEC_T, DC:2 * DC]).then_inc(st_sent, 16)
                act.dma_start(new_pool_sample[0, s, PBUF - DEC_T:PBUF, :],
                              stage[s * DEC_T:(s + 1) * DEC_T, 3 * DC:4 * DC]).then_inc(st_sent, 16)

            act.wait_ge(centred, 1)
            act.activation(gateT, vT, ACT.Square).then_inc(vsq, 1)
            act.wait_ge(var_done, 1)
            act.activation(rms[:, :], ps[:, 5, 0:NT], ACT.Sqrt, bias=epsc[:, :]).then_inc(vrms, 1)
            for c in range(CT_):
                act.wait_ge(ln_ready, c + 1)
                act.activation(gateT[:, c, :], vT[:, c, :], ACT.Sigmoid).then_inc(ln_sig, 1)

            for k in range(KT):
                act.wait_ge(x2_out, k + 1)
                act.activation(sq[:, k, :], xT[:, k, :], ACT.Square).then_inc(sq2, 1)
            act.wait_ge(stat2, 1)
            act.activation(rms[:, :], ps[:, 4, 0:NT], ACT.Sqrt, bias=epsc[:, :]).then_inc(rms2, 1)

            act.wait_ge(st_sent, 16 * (2 + 2 * DEC_B))
            for j, (_, n) in enumerate(TOK_TILES):
                for half in range(2):
                    i = 2 * j + half
                    act.wait_ge(h2_turned, i + 1)
                    act.copy(rows[0:n, j, half * BANK:(half + 1) * BANK],
                             ps[0:n, (0, 1, 2, 3, 4, 7)[i], :]).then_inc(h2_out, 1)
            act.wait_ge(shifted, 1)
            act.activation(wgt[:, :, :], lg[:, :, :], ACT.Exp).then_inc(expd, 1)
            for t in range(KT):
                act.wait_ge(bd_done, t + 1)
                act.copy(accT[:, t, :], ps[:, BD_BANKS[t % 4], 0:NT]).then_inc(bd_out, 1)

            def gather_out(g):
                act.wait_ge(gathered, g)
                act.copy(hgT, ps[:, HG_BANK:HG_BANK + 2, :]
                         .rearrange("p b (k s) -> p (b k) s", s=SLOTS)).then_inc(hg_out, 1)

            def turned_out(r):
                for half in range(2):
                    act.wait_ge(y_turned, 2 * r + half + 1)
                    act.copy(yrow[:, half * BANK:(half + 1) * BANK],
                             ps[:, T_BANK + half, :]).then_inc(yrow_out, 1)

            def expert_pass(n0, p):
                gather_out(p * GAT + 1)
                with act.Fori(0, NE) as e:
                    n = n0 + e
                    for h in range(2):
                        act.wait_ge(chunk_used, NMIX + n * EXPERT_CHUNKS + 2 * h + 2)
                        for m in range(4):
                            ins = act.activation(lin[:, h, m * SLOTS:(m + 1) * SLOTS],
                                                 ps[:, UP_BANKS[2 * h + 1], m * SLOTS:(m + 1) * SLOTS],
                                                 ACT.Identity, bias=bupT[:, KT + 4 * h + m, bass.ds(e, 1)])
                        ins.then_inc(lin_out, 1)
                        act.wait_ge(glu_out, 2 * n + h + 1)
                        act.activation(sig[:, h, :], glu[:, h, :], ACT.Sigmoid, scale=ALPHA)\
                            .then_inc(sig_out, 1)
                    turned_out(p * GAT + e)
                    gather_out(p * GAT + e + 2)
                    for h in range(2):
                        act.wait_ge(chunk_used, NMIX + n * EXPERT_CHUNKS + 5 + h)
                        act.copy(ysT[:, 4 * h:4 * h + 4, :],
                                 ps[:, UP_BANKS[4 + h], :].rearrange("p (k s) -> p k s", s=SLOTS))\
                            .then_inc(y_out, 1)
                turned_out(p * GAT + NE)

            expert_pass(0, 0)
            most = act.value_load(cnti[0:1, NE + 1:NE + 2], min_val=0, max_val=NT)
            with act.If(most > SLOTS):
                with act.Fori(1, PASSES) as p:
                    expert_pass(p * NE, p)

            for k in range(KT):
                act.wait_ge(x3_out, k + 1)
                act.activation(sq[:, k, :], xT[:, k, :], ACT.Square).then_inc(sq3, 1)
            act.wait_ge(stat3, 1)
            act.activation(rms[:, :], ps[:, 0, 0:NT], ACT.Sqrt, bias=epsc[:, :]).then_inc(rms3, 1)
            for j, (_, n) in enumerate(TOK_TILES):
                for half in range(2):
                    i = 2 * j + half
                    act.wait_ge(fin_turned, i + 1)
                    act.copy(rows[0:n, j, half * BANK:(half + 1) * BANK], ps[0:n, 1 + i, :])\
                        .then_inc(fin_out, 1)

        @block.vector
        def _(dve):
            step = [0]

            def link(ins):
                step[0] += 1
                ins.then_inc(dve_done, 1)
                dve.wait_ge(dve_done, step[0])

            V = nc.vector
            V.memset(uf_p[:, :, 0:CBUF], 0.0).then_inc(dve_done, 1)
            V.memset(rankm[:, :, NE:NE + 1], -1.0).then_inc(dve_done, 1)
            V.memset(cntf[:, :], 0.0).then_inc(dve_done, 1)
            step[0] = 3

            for g in range(17):
                dve.wait_ge(turned, g + 1)
                bank = ps[:, g % 8, :]
                if g == 0:
                    ins = V.tensor_copy(vec[:, 0:NVEC], bank[:, 0:NVEC])
                elif g < 9:
                    ins = V.tensor_copy(xT[:, g - 1, :], bank[:, 0:NT])
                elif g == 9:
                    ins = V.tensor_copy(silc[:, :, :], bank[:, 0:KT * SEQS].rearrange("p (k s) -> p k s", k=KT))
                elif g == 10:
                    ins = V.tensor_copy(taps[:, :, :], bank[:, 0:CT_ * TAPS].rearrange("p (c w) -> p c w", c=CT_))
                elif g < 15:
                    ins = V.tensor_copy(uf_s[:, g - 11, :, 0:CBUF],
                                        bank[:, 0:DEC_B * CBUF].rearrange("p (s t) -> p s t", t=CBUF))
                elif g == 15:
                    for c in range(CT_):
                        ins = V.tensor_copy(pool_bufs[0][1][:, c, :, 0:PBUF],
                                            bank[:, c * 120:(c + 1) * 120].rearrange("p (s t) -> p s t", t=PBUF))
                else:
                    ins = V.tensor_copy(bupT[:, :, :], bank.rearrange("p (n e) -> p n e", e=NE))
                ins.then_inc(turn_out, 1)
                if g == 0:
                    dve.wait_ge(silu_c, 1)
                    V.tensor_tensor(c_rows.rearrange("p (k n) -> p k n", k=4),
                                    c_rows.rearrange("p (k n) -> p k n", k=4),
                                    sq[0:SEQS, 0:4, 0:256], ALU.mult).then_inc(silu_c, 1)

            dve.wait_ge(consts, 11)
            link(V.reciprocal(icnt[:, :, :], icnt[:, :, :]))

            def mod_out(first, last, bank, at):
                a = VEC_ROWS["b_ada"][0]
                n = last - first
                link(V.tensor_tensor(modT[:, first:last, :],
                                     ps[:, bank, at:at + n * SEQS].rearrange("p (k s) -> p k s", s=SEQS),
                                     vec[:, a + first:a + last].unsqueeze(2).to_broadcast([P, n, SEQS]), ALU.add))

            def gain(sc, norm):
                part = modT[:, sc * KT:(sc + 1) * KT, :]
                link(V.tensor_scalar(part, part, 1.0, None, ALU.add))
                link(V.tensor_tensor(part, part, vcols(norm).unsqueeze(2).to_broadcast([P, KT, SEQS]), ALU.mult))

            def per_seq(i):
                return modT[:, i * KT:(i + 1) * KT, 1:SEQS].unsqueeze(3).to_broadcast([P, KT, DEC_B, DEC_T])

            def modulate(sh, sc, ready):
                link(V.reciprocal(rstd[:, :], rms[:, :]))
                link(V.tensor_tensor(hT[:, :, :], xT[:, :, :],
                                     rstd[:, :].unsqueeze(1).to_broadcast([P, KT, NT]), ALU.mult))
                link(V.tensor_tensor(decoded(hT), decoded(hT), per_seq(sc), ALU.mult))
                link(V.tensor_tensor(decoded(hT), decoded(hT), per_seq(sh), ALU.add))
                for k in range(KT):
                    V.tensor_scalar(hT[:, k, 0:SEQ], hT[:, k, 0:SEQ], modT[:, sc * KT + k, 0:1],
                                    modT[:, sh * KT + k, 0:1], ALU.mult, ALU.add).then_inc(ready, 1)

            dve.wait_ge(turn_out, 17)
            dve.wait_ge(chunk_used, 4)
            mod_out(0, 2 * KT, 2, 0)
            gain(1, "norm_mix")
            dve.wait_ge(rms1, 1)
            modulate(0, 1, h1)

            for c in range(CT_):
                dve.wait_ge(z_out, CT_ + c + 1)
                V.tensor_tensor(uT[:, c, :], uT[:, c, :], gateT[:, c, :], ALU.mult).then_inc(u_ready, 1)
            for c in range(CT_):
                dve.wait_ge(u_ready, c + 1)
                V.tensor_copy(uf_p[:, c, CBUF:CBUF + SEQ], uT[:, c, 0:SEQ]).then_inc(uf_ready, 1)
                V.tensor_copy(uf_s[:, c, :, CBUF:CBUF + DEC_T],
                              uT[:, c, SEQ:NT].rearrange("p (s t) -> p s t", t=DEC_T)).then_inc(uf_ready, 1)
            dve.wait_ge(uf_ready, 2 * CT_)
            for w in range(TAPS):
                for c in range(CT_):
                    for q, (out, hist) in enumerate((
                            (vT[:, c, 0:SEQ], uf_p[:, c, w:w + SEQ]),
                            (vT[:, c, SEQ:NT].rearrange("p (s t) -> p s t", t=DEC_T),
                             uf_s[:, c, :, w:w + DEC_T]))):
                        tap = taps[:, c, w:w + 1]
                        if w == 0:
                            V.tensor_scalar(out, hist, tap, vcol("conv_b", c), ALU.mult, ALU.add)\
                                .then_inc(v_ready, 1)
                        else:
                            dve.wait_ge(v_ready, 2 * CT_ * (w - 1) + 2 * c + q + 1)
                            V.scalar_tensor_tensor(out=out, in0=hist, scalar=tap, in1=out,
                                                   op0=ALU.mult, op1=ALU.add).then_inc(v_ready, 1)

            dve.wait_ge(pool_step, 2 + 2 * CT_ + 10)
            dve.wait_ge(st_turned, 4)
            for g, w in enumerate(WINDOWS):
                s_p, s_s = pool_bufs[1 + g % 2]
                early = s_p[:, g, PBUF:PBUF + 16]
                V.tensor_tensor(early, early, icnt[:, g, :], ALU.mult).then_inc(pooled, 1)
                V.scalar_tensor_tensor(out=upT[:, g, 16:SEQ], in0=s_p[:, g, PBUF + 16:PBUF + SEQ],
                                       scalar=1.0 / w, in1=upT[:, g, 16:SEQ],
                                       op0=ALU.mult, op1=ALU.subtract).then_inc(pooled, 1)
                dec = upT[:, g, SEQ:NT].rearrange("p (s t) -> p s t", t=DEC_T)
                V.scalar_tensor_tensor(out=dec, in0=s_s[:, g, :, PBUF:PBUF + DEC_T], scalar=1.0 / w,
                                       in1=dec, op0=ALU.mult, op1=ALU.subtract).then_inc(pooled, 1)
                dve.wait_ge(pooled, 4 * g + 1)
                V.tensor_tensor(upT[:, g, 0:16], early, upT[:, g, 0:16], ALU.subtract).then_inc(pooled, 1)

            dve.wait_ge(v_ready, 2 * CT_ * TAPS)
            dve.wait_ge(mean_done, 1)
            V.tensor_tensor(vT, vT, ps[:, 4, 0:NT].unsqueeze(1).to_broadcast([P, CT_, NT]), ALU.subtract)\
                .then_inc(centred, 1)
            dve.wait_ge(vrms, 1)
            link(V.reciprocal(rstd[:, :], rms[:, :]))
            dve.wait_ge(centred, 1)
            link(V.tensor_tensor(vT, vT, rstd[:, :].unsqueeze(1).to_broadcast([P, CT_, NT]), ALU.mult))
            for c in range(CT_):
                V.tensor_scalar(vT[:, c, :], vT[:, c, :], vcol("conv_ln_g", c), vcol("conv_ln_b", c),
                                ALU.mult, ALU.add).then_inc(ln_ready, 1)
            for c in range(CT_):
                dve.wait_ge(ln_sig, c + 1)
                V.tensor_tensor(vT[:, c, :], vT[:, c, :], gateT[:, c, :], ALU.mult).then_inc(vact, 1)

            dve.wait_ge(z_out, 28)
            for t in range(KT):
                dve.wait_ge(yp_done, t + 1)
                V.scalar_tensor_tensor(out=sgT[:, KT + t, :], in0=ps[:, t % 4, 0:NT],
                                       scalar=vcol("pool_scale", t), in1=sgT[:, KT + t, :],
                                       op0=ALU.mult, op1=ALU.mult).then_inc(yp_out, 1)
            dve.wait_ge(chunk_used, MIX_AT["ada", 5] + 1)
            mod_out(2 * KT, 3 * KT, 6, 0)
            for t in range(KT):
                dve.wait_ge(yc_done, t + 1)
                link(V.tensor_tensor(sgT[:, t, :], ps[:, t % 4, 0:NT], sgT[:, t, :], ALU.mult))
                V.tensor_tensor(hT[:, t, :], sgT[:, t, :], sgT[:, KT + t, :], ALU.add).then_inc(m_ready, 1)
            def residual(t, y, gt, done):
                link(V.tensor_tensor(y[1], y[1], modT[:, gt * KT + t, 1:SEQS].unsqueeze(2)
                                     .to_broadcast([P, DEC_B, DEC_T]), ALU.mult) if y[2] is None else
                     V.tensor_tensor(y[2], y[1], modT[:, gt * KT + t, 1:SEQS].unsqueeze(2)
                                     .to_broadcast([P, DEC_B, DEC_T]), ALU.mult))
                V.scalar_tensor_tensor(out=xT[:, t, 0:SEQ], in0=y[0], scalar=modT[:, gt * KT + t, 0:1],
                                       in1=xT[:, t, 0:SEQ], op0=ALU.mult, op1=ALU.add)
                xs = xT[:, t, SEQ:NT].rearrange("p (s t) -> p s t", t=DEC_T)
                V.tensor_tensor(xs, xs, y[1] if y[2] is None else y[2], ALU.add).then_inc(done, 1)

            for t in range(KT):
                dve.wait_ge(yo_done, t + 1)
                tmp = rstd[:, t * DEC:(t + 1) * DEC].rearrange("p (s t) -> p s t", t=DEC_T)
                residual(t, (ps[:, t % 4, 0:SEQ],
                             ps[:, t % 4, SEQ:NT].rearrange("p (s t) -> p s t", t=DEC_T), tmp), 2, x2_out)
            dve.wait_ge(chunk_used, MIX_AT["ada", 9] + 1)
            mod_out(3 * KT, 5 * KT, 7, 0)
            gain(4, "norm_ffn")
            dve.wait_ge(rms2, 1)
            dve.wait_ge(x2_out, KT)
            modulate(3, 4, h2)
            dve.wait_ge(chunk_used, NMIX)
            mod_out(5 * KT, 6 * KT, 6, 0)

            link(V.memset(lg[:, :, :], 0.0))
            dve.wait_ge(logits, 1)
            dve.wait_ge(ld_late, 48)
            for j, (_, n) in enumerate(TOK_TILES):
                ins = V.tensor_tensor(lg[0:n, j, :], ps[0:n, 5, j * NE:(j + 1) * NE], brout[0:n, :], ALU.add)
            link(ins)
            for j in range(NJ):
                ins = V.max(out=top8[:, j, :], in_=lg[:, j, :])
            link(ins)
            fourth = top8[:, :, TOPK - 1:TOPK].to_broadcast([P, NJ, NE])
            V.tensor_tensor(mask[:, :, :], lg[:, :, :], fourth, ALU.is_gt)
            link(V.tensor_tensor(eq[:, :, :], lg[:, :, :], fourth, ALU.is_equal))
            V.tensor_tensor(lg[:, :, :], lg[:, :, :], top8[:, :, 0:1].to_broadcast([P, NJ, NE]),
                            ALU.subtract).then_inc(shifted, 1)
            V.tensor_reduce(need[:, :], mask[:, :, :], AX.X, ALU.add)
            onesv = ones[:, 0:NE]
            for j in range(NJ):
                ins = V.tensor_tensor_scan(cum[:, j, :], onesv, eq[:, j, :], 0.0, ALU.mult, ALU.add)
            link(ins)
            link(V.tensor_tensor(cum[:, :, :], cum[:, :, :], need[:, :].unsqueeze(2)
                                 .to_broadcast([P, NJ, NE]), ALU.add))
            link(V.scalar_tensor_tensor(out=eq[:, :, :], in0=cum[:, :, :], scalar=float(TOPK) + 0.5,
                                        in1=eq[:, :, :], op0=ALU.is_lt, op1=ALU.mult))
            link(V.tensor_tensor(mask[:, :, :], mask[:, :, :], eq[:, :, :], ALU.add))
            V.memset(mask[DEC:2 * DEC, NJ - 1, :], 0.0)
            V.memset(mask[2 * DEC:P, NJ - 1, :], 0.0).then_inc(mask_ready, 1)
            dve.wait_ge(mask_ready, 1)
            dve.wait_ge(expd, 1)
            link(V.tensor_tensor(wgt[:, :, :], wgt[:, :, :], mask[:, :, :], ALU.mult))
            link(V.tensor_reduce(need[:, :], wgt[:, :, :], AX.X, ALU.add))
            link(V.tensor_scalar(need[:, :], need[:, :], 1e-30, None, ALU.max))
            link(V.reciprocal(need[:, :], need[:, :]))
            V.tensor_tensor(wgt[:, :, :], wgt[:, :, :], need[:, :].unsqueeze(2)
                            .to_broadcast([P, NJ, NE]), ALU.mult).then_inc(wgt_ready, 1)
            dve.wait_ge(ranked, 1)
            rk = ps[:, 6, 0:NJ * NE].rearrange("p (j e) -> p j e", e=NE)
            link(V.scalar_tensor_tensor(out=eq[:, :, :], in0=rk, scalar=1.0, in1=mask[:, :, :],
                                        op0=ALU.add, op1=ALU.mult))
            link(V.tensor_scalar(rankm[:, :, 0:NE], eq[:, :, :], -1.0, None, ALU.add))
            link(V.tensor_copy(cntf[:, 0:NE], ps[0:1, 6, NJ * NE:(NJ + 1) * NE]))
            link(V.tensor_reduce(cntf[:, NE + 1:NE + 2], cntf[:, 0:NE], AX.X, ALU.max))
            V.tensor_copy(cnti[:, :], cntf[:, :]).then_inc(rank_ready, 1)
            dve.wait_ge(wT_turned, 1)
            V.tensor_copy(wT[:, :], ps[0:NE, 5, 0:NT]).then_inc(wT_out, 1)
            dve.wait_ge(wT_out, 1)
            dve.wait_ge(h2_out, 6)
            V.memset(ps[:, HG_BANK:HG_BANK + 2, :], 0.0).then_inc(hg_clear, 1)
            dve.wait_ge(bd_out, KT)
            V.memset(ps[:, 0:3, :], 0.0).then_inc(added, 1)
            V.memset(ysT, 0.0).then_inc(y_out, 1)

            def hot_for(e):
                for j in range(NJ):
                    ins = V.tensor_scalar(hot[:, j, :], iota[:, :], rankm[:, j, bass.ds(e, 1)], None,
                                          ALU.is_equal)
                ins.then_inc(hot_ready, 1)

            def expert_pass(n0, p):
                dve.wait_ge(pass_ready, p + 1)
                hot_for(0)
                V.memset(comb, 0.0).then_inc(comb_out, 1)
                with dve.Fori(0, NE) as e:
                    n = n0 + e
                    dve.wait_ge(gathered, p * GAT + e + 1)
                    hot_for(e + 1)
                    for j in range(NJ):
                        ins = V.tensor_scalar(hotw[:, j, :], iota[:, :], rankm[:, j, bass.ds(e, 1)],
                                              wgt[:, j, bass.ds(e, 1)], ALU.is_equal, ALU.mult)
                    ins.then_inc(hotw_ready, 1)
                    for h in range(2):
                        dve.wait_ge(chunk_used, NMIX + n * EXPERT_CHUNKS + 2 * h + 1)
                        for m in range(4):
                            ins = V.tensor_scalar(glu[:, h, m * SLOTS:(m + 1) * SLOTS],
                                                  ps[:, UP_BANKS[2 * h], m * SLOTS:(m + 1) * SLOTS],
                                                  bupT[:, 4 * h + m, bass.ds(e, 1)], LIMIT,
                                                  ALU.add, ALU.min)
                        ins.then_inc(glu_out, 1)
                        dve.wait_ge(lin_out, 2 * n + h + 1)
                        V.tensor_scalar(lin[:, h, :], lin[:, h, :], LIMIT, -LIMIT, ALU.min, ALU.max)\
                            .then_inc(lin_clip, 1)
                        dve.wait_ge(sig_out, 2 * n + h + 1)
                        dve.wait_ge(glu_out, 2 * n + h + 1)
                        V.tensor_tensor(glu[:, h, :], glu[:, h, :], sig[:, h, :], ALU.mult)\
                            .then_inc(gs_out, 1)
                        dve.wait_ge(lin_clip, 2 * n + h + 1)
                        dve.wait_ge(gs_out, 2 * n + h + 1)
                        V.scalar_tensor_tensor(out=oT[:, 4 * h:4 * h + 4, :],
                                               in0=lin[:, h, :].rearrange("p (k s) -> p k s", s=SLOTS),
                                               scalar=1.0,
                                               in1=glu[:, h, :].rearrange("p (k s) -> p k s", s=SLOTS),
                                               op0=ALU.add, op1=ALU.mult).then_inc(o_ready, 1)
                    add_results(p * GAT + e)
                    dve.wait_ge(comb_turned, n + 1)
                    V.tensor_copy(comb, ps[:, T_BANK + 2, 0:NT]).then_inc(comb_out, 1)
                add_results(p * GAT + NE)

            def add_results(r):
                for k in range(KT):
                    dve.wait_ge(combined, KT * r + k + 1)
                    dve.wait_ge(added, KT * r + 1)
                    V.tensor_tensor(accT[:, k, :], accT[:, k, :], ps[:, T_BANK + k % 3, 0:NT], ALU.add)\
                        .then_inc(added, 1)

            V.memset(need[:, :], 0.0).then_inc(pass_ready, 1)
            expert_pass(0, 0)
            dve.wait_ge(added, KT * GAT + 1)
            most = dve.value_load(cnti[0:1, NE + 1:NE + 2], min_val=0, max_val=NT)
            with dve.If(most > SLOTS):
                with dve.Fori(1, PASSES) as p:
                    dve.wait_ge(hotw_ready, p * NE)
                    dve.wait_ge(hot_ready, p * GAT)
                    V.tensor_scalar(rankm[:, :, :], rankm[:, :, :], float(-SLOTS), None, ALU.add)\
                        .then_inc(pass_ready, 1)
                    expert_pass(p * NE, p)
                    dve.wait_ge(added, (p + 1) * (KT * GAT) + 1)

            for t in range(KT):
                residual(t, (accT[:, t, 0:SEQ],
                             accT[:, t, SEQ:NT].rearrange("p (s t) -> p s t", t=DEC_T), None), 5, x3_out)
            dve.wait_ge(rms3, 1)
            link(V.reciprocal(rstd[:, :], rms[:, :]))
            dve.wait_ge(x3_out, KT)
            for t in range(KT):
                V.scalar_tensor_tensor(out=hT[:, t, :], in0=xT[:, t, :], scalar=vcol("norm_final", t),
                                       in1=rstd[:, :], op0=ALU.mult, op1=ALU.mult).then_inc(yn, 1)

        @block.tensor
        def _(pe):
            def chunk(c, k):
                return ring[:, c % RING, :].rearrange("p (k n) -> p k n", k=k)

            def chunk_landed(c):
                pe.wait_ge(landed[c % RING], 16 * (c // RING + 1))

            pe.wait_ge(consts, 6)
            for g in range(17):
                bank = ps[:, g % 8, :]
                if g >= 8:
                    pe.wait_ge(turn_out, g - 7)
                if g == 0:
                    pe.wait_ge(ld_vec, 16 * len(VEC_ROWS))
                    ins = pe.transpose(bank[:, 0:NVEC], vec_rows[0:NVEC, :], ident[0:NVEC, 0:NVEC])
                elif g < 9:
                    pe.wait_ge(ld_x, 32)
                    for j, (t0, n) in enumerate(TOK_TILES):
                        ins = pe.transpose(bank[:, t0:t0 + n], rows[0:n, j, (g - 1) * P:g * P],
                                           ident[0:n, 0:n])
                elif g == 9:
                    pe.wait_ge(silu_c, 2)
                    for k in range(KT):
                        ins = pe.transpose(bank[:, k * SEQS:(k + 1) * SEQS], c_rows[:, k * P:(k + 1) * P],
                                           ident[0:SEQS, 0:SEQS])
                elif g == 10:
                    pe.wait_ge(ld_taps, 16)
                    for c in range(CT_):
                        ins = pe.transpose(bank[:, c * TAPS:(c + 1) * TAPS], tap_rows[:, c * P:(c + 1) * P],
                                           ident[0:TAPS, 0:TAPS])
                elif g < 15:
                    pe.wait_ge(ld_state, 32)
                    for j in range(2):
                        ins = pe.transpose(bank[:, j * 120:(j + 1) * 120],
                                           sconv_rows[:, j, (g - 11) * P:(g - 10) * P], ident[0:120, 0:120])
                elif g == 15:
                    for c in range(CT_):
                        ins = pe.transpose(bank[:, c * 120:(c + 1) * 120], spool_rows[:, c * P:(c + 1) * P],
                                           ident[0:120, 0:120])
                else:
                    pe.wait_ge(ld_bup, 16)
                    for t in range(2 * KT):
                        ins = pe.transpose(bank[:, t * NE:(t + 1) * NE], bup_rows[:, t * P:(t + 1) * P],
                                           ident[0:NE, 0:NE])
                ins.then_inc(turned, 1)

            def channel_sums(bank, src, weight, tiles, ready, done):
                for k in range(tiles):
                    if ready is not None:
                        pe.wait_ge(ready, k + 1)
                    ins = pe.matmul(ps[:, bank, 0:NT], avg[:, weight, :], src[:, k, :],
                                    start=(k == 0), stop=(k == tiles - 1))
                ins.then_inc(done, 1)

            def modulation(i, bank, first):
                c = MIX_AT["ada", i]
                w = chunk(c, KT)
                chunk_landed(c)
                for m in range(4):
                    at = (4 * i + m - first) * SEQS
                    for k in range(KT):
                        ins = pe.matmul(ps[:, bank, at:at + SEQS], w[:, k, m * P:(m + 1) * P],
                                        silc[:, k, :], start=(k == 0), stop=(k == KT - 1))
                ins.then_inc(chunk_used, 1)

            pe.wait_ge(turn_out, 11)
            channel_sums(1, sq, 0, KT, sq1, stat1)
            for i in range(4):
                modulation(i, 2, 0)

            pe.wait_ge(h1, KT)
            for i in range(7):
                c = MIX_AT["in", i]
                w = chunk(c, KT)
                chunk_landed(c)
                for m in range(4):
                    t = 4 * i + m
                    if t >= 8:
                        pe.wait_ge(z_out, t - 7)
                    for k in range(KT):
                        ins = pe.matmul(ps[:, t % 8, 0:NT], w[:, k, m * P:(m + 1) * P], hT[:, k, :],
                                        start=(k == 0), stop=(k == KT - 1))
                    ins.then_inc(z_done, 1)
                pe.wait_ge(z_done, 4 * i + 4)
                pe.sem_inc(chunk_used, 1)

            pe.wait_ge(u_ready, CT_)
            for i, (src, t0, t1) in enumerate(((uT, SEQ - CBUF, SEQ), (uT, SEQ, NT),
                                               (upT, SEQ - PBUF, SEQ), (upT, SEQ, NT))):
                pe.wait_ge(z_out, 25 + i)
                for c in range(CT_):
                    ins = pe.transpose(ps[0:t1 - t0, i, c * P:(c + 1) * P], src[:, c, t0:t1], ident[:, :])
                ins.then_inc(st_turned, 1)

            pe.wait_ge(v_ready, 2 * CT_ * TAPS)
            channel_sums(4, vT, 1, CT_, None, mean_done)
            modulation(4, 6, 16)
            pe.wait_ge(vsq, 1)
            channel_sums(5, gateT, 1, CT_, None, var_done)
            modulation(5, 6, 16)

            pe.wait_ge(ld_late, 48)
            pe.wait_ge(pooled, 4 * CT_)
            for t in range(KT):
                if t < 4:
                    pe.wait_ge(st_out, t + 1)
                else:
                    pe.wait_ge(yp_out, t - 3)
                pe.matmul(ps[:, t % 4, 0:NT], wpool[:, t // 2, (t % 2) * P:(t % 2 + 1) * P], upT[:, t // 2, :],
                          start=True, stop=True).then_inc(yp_done, 1)

            c = MIX_AT["conv_out", 0]
            w = chunk(c, CT_)
            chunk_landed(c)
            pe.wait_ge(vact, CT_)
            for t in range(KT):
                if t < 4:
                    pe.wait_ge(yp_out, t + 5)
                else:
                    pe.wait_ge(m_ready, t - 3)
                for k in range(CT_):
                    ins = pe.matmul(ps[:, t % 4, 0:NT], w[:, k, t * P:(t + 1) * P], vT[:, k, :],
                                    start=(k == 0), stop=(k == CT_ - 1))
                ins.then_inc(yc_done, 1)
            pe.wait_ge(yc_done, KT)
            pe.sem_inc(chunk_used, 1)
            modulation(6, 7, 24)
            modulation(7, 7, 24)

            pe.wait_ge(m_ready, KT)
            for i in range(2):
                c = MIX_AT["out", i]
                w = chunk(c, KT)
                chunk_landed(c)
                for m in range(4):
                    t = 4 * i + m
                    if t >= 4:
                        pe.wait_ge(x2_out, t - 3)
                    for k in range(KT):
                        ins = pe.matmul(ps[:, t % 4, 0:NT], w[:, k, m * P:(m + 1) * P], hT[:, k, :],
                                        start=(k == 0), stop=(k == KT - 1))
                    ins.then_inc(yo_done, 1)
                pe.wait_ge(yo_done, 4 * i + 4)
                pe.sem_inc(chunk_used, 1)
            modulation(8, 7, 24)
            modulation(9, 7, 24)
            channel_sums(4, sq, 0, KT, sq2, stat2)
            modulation(10, 6, 40)
            modulation(11, 6, 40)

            pe.wait_ge(h2, KT)
            for j, (t0, n) in enumerate(TOK_TILES):
                for k in range(KT):
                    ins = pe.matmul(ps[0:n, 5, j * NE:(j + 1) * NE], hT[:, k, t0:t0 + n], wrouter[:, k, :],
                                    start=(k == 0), stop=(k == KT - 1))
            ins.then_inc(logits, 1)
            for j, (t0, n) in enumerate(TOK_TILES):
                for half in range(2):
                    i = 2 * j + half
                    for q in range(4):
                        k = 4 * half + q
                        ins = pe.transpose(ps[0:n, (0, 1, 2, 3, 4, 7)[i], q * P:(q + 1) * P],
                                           hT[:, k, t0:t0 + n], ident[:, :])
                    ins.then_inc(h2_turned, 1)
            pe.wait_ge(mask_ready, 1)
            for j in range(NJ):
                for i in range(j + 1):
                    pe.matmul(ps[:, 6, j * NE:(j + 1) * NE], upper[:, :] if i == j else ones[:, :],
                              mask[:, i, :], start=(i == 0), stop=(i == j))
            for i in range(NJ):
                ins = pe.matmul(ps[:, 6, NJ * NE:(NJ + 1) * NE], ones[:, :], mask[:, i, :],
                                start=(i == 0), stop=(i == NJ - 1))
            ins.then_inc(ranked, 1)
            pe.wait_ge(wgt_ready, 1)
            for j, (t0, n) in enumerate(TOK_TILES):
                ins = pe.transpose(ps[0:NE, 5, t0:t0 + n], wgt[0:n, j, :], ident[0:n, 0:n])
            ins.then_inc(wT_turned, 1)
            pe.wait_ge(wT_out, 1)
            pe.wait_ge(h2_out, 6)
            pe.wait_ge(ld_bdown, 16)
            for t in range(KT):
                if t >= 4:
                    pe.wait_ge(bd_out, t - 3)
                pe.matmul(ps[:, BD_BANKS[t % 4], 0:NT], bdown[:, t * P:(t + 1) * P], wT[:, :],
                          start=True, stop=True).then_inc(bd_done, 1)

            def by_width(count, emit):
                with pe.If(count > WIDTHS[1]):
                    emit(SLOTS)
                with pe.Else():
                    with pe.If(count > WIDTHS[0]):
                        emit(WIDTHS[1])
                    with pe.Else():
                        emit(WIDTHS[0])

            def gather(g, width):
                for k in range(KT):
                    for j, (_, n) in enumerate(TOK_TILES):
                        at = (k % 4) * SLOTS
                        ins = pe.matmul(ps[:, HG_BANK + k // 4, at:at + width], rows[0:n, j, k * P:(k + 1) * P],
                                        hot[0:n, j, 0:width], start=(j == 0), stop=(j == NJ - 1))
                ins.then_inc(gathered, 1)

            def products(n, j, x, width):
                w = chunk(NMIX + j, KT)
                for m in range(4):
                    for k in range(KT):
                        ins = pe.matmul(ps[:, UP_BANKS[j], m * SLOTS:m * SLOTS + width],
                                        w[:, k, m * P:(m + 1) * P], x[:, k, 0:width],
                                        start=(k == 0), stop=(k == KT - 1))
                ins.then_inc(chunk_used, 1)

            def expert_chunk_landed(n, j):
                c = NMIX + j
                pe.wait_ge(landed[c % RING], n * 16 + 16 * (c // RING + 1))

            def up(n, width):
                for j in range(4):
                    expert_chunk_landed(n, j)
                    if j == 3:
                        pe.wait_ge(glu_out, 2 * n + 1)
                    products(n, j, hgT, width)

            def down(n, width):
                for j in (4, 5):
                    expert_chunk_landed(n, j)
                    if j == 4:
                        pe.wait_ge(lin_out, 2 * n + 1)
                    else:
                        pe.wait_ge(glu_out, 2 * n + 2)
                    products(n, j, oT, width)

            def turn_results(r):
                pe.wait_ge(added, KT * r + 1)
                for k in range(KT):
                    ins = pe.transpose(ps[:, T_BANK + k // 4, (k % 4) * P:(k % 4 + 1) * P], ysT[:, k, :],
                                       ident[:, :])
                    if k % 4 == 3:
                        ins.then_inc(y_turned, 1)

            def combine(r, c):
                pe.wait_ge(yrow_out, 2 * r + 2)
                pe.wait_ge(comb_out, c)
                for k in range(KT):
                    if k >= 3:
                        pe.wait_ge(added, KT * r + k - 1)
                    pe.matmul(ps[:, T_BANK + k % 3, 0:NT], yrow[:, k * P:(k + 1) * P], comb,
                              start=True, stop=True).then_inc(combined, 1)

            def expert_pass(n0, p, fixed):
                def sized(count, emit):
                    if fixed:
                        emit(SLOTS)
                    else:
                        by_width(count, emit)

                pe.wait_ge(hot_ready, p * GAT + 1)
                gather(0, SLOTS)
                with pe.Fori(0, NE) as e:
                    n = n0 + e
                    this = nxt = None
                    if not fixed:
                        this = pe.value_load(cnti[0:1, bass.ds(e, 1)], min_val=0, max_val=NT)
                        nxt = pe.value_load(cnti[0:1, bass.ds(e + 1, 1)], min_val=0, max_val=NT)
                    pe.wait_ge(hg_out, p * GAT + e + 1)
                    pe.wait_ge(y_out, 2 * n + 1)
                    sized(this, lambda width: up(n, width))
                    turn_results(p * GAT + e)
                    pe.wait_ge(hot_ready, p * GAT + e + 2)
                    sized(nxt, lambda width: gather(0, width))
                    combine(p * GAT + e, p * GAT + e + 1)
                    pe.wait_ge(hotw_ready, n + 1)
                    pe.wait_ge(added, KT * (p * GAT + e) + 7)
                    for j, (t0, nt) in enumerate(TOK_TILES):
                        ins = pe.transpose(ps[:, T_BANK + 2, t0:t0 + nt], hotw[0:nt, j, :], ident[0:nt, 0:nt])
                    ins.then_inc(comb_turned, 1)
                    pe.wait_ge(o_ready, 2 * n + 2)
                    sized(this, lambda width: down(n, width))
                pe.wait_ge(y_out, 2 * n0 + 2 * NE + 1)
                turn_results(p * GAT + NE)
                combine(p * GAT + NE, p * GAT + NE + 1)

            pe.wait_ge(hg_clear, 1)
            pe.wait_ge(added, 1)
            expert_pass(0, 0, False)
            most = pe.value_load(cnti[0:1, NE + 1:NE + 2], min_val=0, max_val=NT)
            with pe.If(most > SLOTS):
                with pe.Fori(1, PASSES) as p:
                    expert_pass(p * NE, p, True)

            channel_sums(0, sq, 0, KT, sq3, stat3)
            pe.wait_ge(yn, KT)
            for j, (t0, n) in enumerate(TOK_TILES):
                for half in range(2):
                    for q in range(4):
                        ins = pe.transpose(ps[0:n, 1 + 2 * j + half, q * P:(q + 1) * P],
                                           hT[:, 4 * half + q, t0:t0 + n], ident[:, :])
                    ins.then_inc(fin_turned, 1)


_INS = ['x_prompt', 'x_sample', 'state_conv', 'state_pool', 'c_prompt', 'c_sample', 'w_ada', 'b_ada',
        'norm_mix', 'w_in', 'b_in', 'conv_w', 'conv_b', 'conv_ln_g', 'conv_ln_b', 'w_conv_out', 'w_pool',
        'pool_scale', 'w_out', 'norm_ffn', 'w_router', 'b_router', 'w_up', 'b_up', 'w_down', 'b_down',
        'norm_final']
_OUTS = [(1, SEQ, D), (DEC_B, DEC_T, D), (1, 1, CBUF, DC), (1, 1, PBUF, DC),
         (1, DEC_B, CBUF, DC), (1, DEC_B, PBUF, DC)]


def kernel(**inputs):
    import numpy as np
    import concourse.bacc as bacc
    from concourse.bass_utils import run_bass_kernel_spmd

    nc = bacc.Bacc("TRN2", target_bir_lowering=False, num_devices=1)
    arrays, args = {}, []
    for name in _INS:
        a = np.ascontiguousarray(inputs[name])
        arrays[f"in_{name}_dram"] = a
        args.append(nc.dram_tensor(f"in_{name}_dram", a.shape, mybir.dt.from_np(a.dtype),
                                   kind="ExternalInput").ap())
    for i, shape in enumerate(_OUTS):
        args.append(nc.dram_tensor(f"out_{i}_dram", shape, F32, kind="ExternalOutput").ap())
    build(nc, *args)
    r = run_bass_kernel_spmd(nc, [arrays], core_ids=[0])
    return tuple(r.results[0][f"out_{i}_dram"] for i in range(len(_OUTS)))
```

```python
from contextlib import ExitStack

import concourse.bass as bass
from concourse import mybir

P = 128
F32 = mybir.dt.float32
I32 = mybir.dt.int32
ALU = mybir.AluOpType
ACT = mybir.ActivationFunctionType
AX = mybir.AxisListType

D = 1024
KT = D // P
SEQ = 256
DEC_B, DEC_T = 8, 4
DEC = DEC_B * DEC_T
NT = SEQ + DEC
SEQS = 1 + DEC_B
TOK_TILES = [(0, P), (P, P), (2 * P, NT - 2 * P)]
NJ = len(TOK_TILES)
DC = D // 2
CT_ = DC // P
TAPS = 31
CBUF = TAPS - 1
WINDOWS = (2, 4, 8, 16)
PBUF = max(WINDOWS) - 1
NE = 32
TOPK = 4
LIMIT = 7.0
ALPHA = 1.702
EPS = 1e-6

SLOTS = 128
WIDTHS = (32, 64)
QW = WIDTHS[0]
NQ = SLOTS // QW
PASSES = (NT + SLOTS - 1) // SLOTS

RING = 6
COLS = 512
BANK = 512

MIXER_CHUNKS = ([("ada", i) for i in range(4)] + [("in", i) for i in range(7)] +
                [("ada", 4), ("ada", 5), ("conv_out", 0), ("ada", 6), ("ada", 7),
                 ("out", 0), ("out", 1)] + [("ada", i) for i in range(8, 12)])
NMIX = len(MIXER_CHUNKS)
MIX_AT = {c: i for i, c in enumerate(MIXER_CHUNKS)}
EXPERT_CHUNKS = 6

VEC_ROWS = {}
_at = 0
for _name, _n in (("b_ada", 48), ("b_in", 28), ("norm_mix", 8), ("norm_ffn", 8), ("norm_final", 8),
                  ("pool_scale", 8), ("conv_b", 4), ("conv_ln_g", 4), ("conv_ln_b", 4)):
    VEC_ROWS[_name] = (_at, _n)
    _at += _n
NVEC = _at

PF_W = (PBUF + SEQ) + DEC_B * (PBUF + DEC_T)
UF_W = (CBUF + SEQ) + DEC_B * (CBUF + DEC_T)


def build(nc, x_prompt, x_sample, state_conv, state_pool, c_prompt, c_sample, w_ada, b_ada, norm_mix,
          w_in, b_in, conv_w, conv_b, conv_ln_g, conv_ln_b, w_conv_out, w_pool, pool_scale, w_out,
          norm_ffn, w_router, b_router, w_up, b_up, w_down, b_down, norm_final,
          y_prompt, y_sample, new_conv_prompt, new_pool_prompt, new_conv_sample, new_pool_sample):
    with ExitStack() as ctx:
        def sb(name, shape, dt=F32):
            return ctx.enter_context(nc.sbuf_tensor(name, shape, dt))

        def sem(name):
            return ctx.enter_context(nc.semaphore(name))

        ring = sb("ring", [P, RING, KT * COLS])
        vec = sb("vec", [P, P])
        taps = sb("taps", [P, CT_, TAPS])
        rows = sb("rows", [P, NJ, D])
        wrouter = sb("wrouter", [P, KT, NE])
        wpool = sb("wpool", [P, CT_, 2 * P])
        xT = sb("xT", [P, KT, NT])
        hT = sb("hT", [P, KT, NT])
        sq = sb("sq", [P, KT, NT])
        uv = sb("uv", [P, KT, NT])
        sg = sb("sg", [P, 2 * KT * NT])
        ufull = sb("ufull", [P, CT_ * UF_W])
        pf = sb("pf", [P, CT_ * PF_W])
        pa = sb("pa", [P, CT_ * PF_W])
        pb = sb("pb", [P, CT_ * PF_W])
        modT = sb("modT", [P, 6 * KT, SEQS])
        silc = sb("silc", [P, KT, SEQS])
        rtab = sb("rtab", [P, NQ, NJ, NE + 1])
        sel = sb("sel", [P, SLOTS])
        ident = sb("ident", [P, P])
        upper = sb("upper", [P, P])
        ones = sb("ones", [P, P])
        avg = sb("avg", [P, 2, P])
        epsc = sb("epsc", [P, 1])
        rms = sb("rms", [P, NT])
        rstd = sb("rstd", [P, NT])
        iota = sb("iota", [P, SLOTS])
        icnt = sb("icnt", [P, CT_, 16])
        brout = sb("brout", [P, NE])
        top8 = sb("top8", [P, NJ, 8])
        need = sb("need", [P, NJ])
        wgt = sb("wgt", [P, NJ, NE])
        rankm = sb("rankm", [P, NJ, NE + 1])
        cntf = sb("cntf", [1, NE + 3])
        cnti = sb("cnti", [1, NE + 3], I32)

        tap_rows = pa[0:TAPS, 0:DC]
        vec_rows = pb[:, 0:P]
        bdown = wpool[0:NE, :, :].rearrange("p g n -> p (g n)")
        wT = pa[0:NE, 0:NT]
        lg, mask, eq, cum = (ufull[:, a:a + NJ * NE].rearrange("p (j e) -> p j e", e=NE)
                             for a in range(2 * NJ * SLOTS + NT, 2 * NJ * SLOTS + NT + 4 * NJ * NE, NJ * NE))

        a = 2 * NJ * SLOTS + NT + 4 * NJ * NE
        starts = ufull[:, a:a + NQ * NE].rearrange("p (q e) -> p q e", e=NE)

        sconv_rows = sg[0:120, 2 * D:2 * D + 2 * DC].rearrange("p (j d) -> p j d", j=2)
        c_rows = sg[0:SEQS, 3 * D:4 * D]
        spool_rows = sg[0:120, 4 * D:4 * D + DC]
        sgT = sg[:, :].rearrange("p (t n) -> p t n", n=NT)
        hgT = sg[:, 0:KT * SLOTS].rearrange("p (k s) -> p k s", s=SLOTS)
        oT = sg[:, KT * SLOTS:2 * KT * SLOTS].rearrange("p (h n) -> p h n", h=2)
        otok = sg[:, 2 * KT * SLOTS:3 * KT * SLOTS].rearrange("p (h n) -> p h n", h=2)
        yrow = sg[:, 3 * KT * SLOTS:4 * KT * SLOTS]
        bup = hT[:, :, :].rearrange("p k n -> p (k n)")[:, 0:2 * D]
        hot = ufull[:, 0:NJ * SLOTS].rearrange("p (j s) -> p j s", s=SLOTS)
        hotw = ufull[:, NJ * SLOTS:2 * NJ * SLOTS].rearrange("p (j s) -> p j s", s=SLOTS)
        comb = ufull[:, 2 * NJ * SLOTS:2 * NJ * SLOTS + NT]
        glu = pf[:, 0:2 * BANK].rearrange("p (h n) -> p h n", h=2)
        sig = pa[:, 0:2 * BANK].rearrange("p (h n) -> p h n", h=2)
        lin = pb[:, 0:2 * BANK].rearrange("p (h n) -> p h n", h=2)
        uf = ufull[:, :].rearrange("p (c n) -> p c n", c=CT_)
        uf_p = uf[:, :, 0:CBUF + SEQ]
        uf_s = uf[:, :, CBUF + SEQ:UF_W].rearrange("p c (s t) -> p c s t", s=DEC_B)
        pool_bufs = []
        for buf in (pf, pa, pb):
            v = buf[:, :].rearrange("p (c n) -> p c n", c=CT_)
            pool_bufs.append((v[:, :, 0:PBUF + SEQ],
                              v[:, :, PBUF + SEQ:PF_W].rearrange("p c (s t) -> p c s t", s=DEC_B)))
        uT = uv[:, 0:CT_, :]
        vT = uv[:, CT_:KT, :]
        accT = uv
        gateT = sq[:, 0:CT_, :]
        upT = sq[:, CT_:KT, :]
        stage = rows[:, :, :].rearrange("p j d -> p (j d)")

        def vcol(name, i):
            return vec[:, VEC_ROWS[name][0] + i:VEC_ROWS[name][0] + i + 1]

        def vcols(name):
            a, n = VEC_ROWS[name]
            return vec[:, a:a + n]

        def decoded(ap):
            return ap[:, :, SEQ:NT].rearrange("p k (s t) -> p k s t", t=DEC_T)

        ps = ctx.enter_context(nc.psum_tensor("ps", [P, 8, BANK], F32))

        ld_vec = sem("ld_vec")
        ld_x = sem("ld_x")
        ld_c = sem("ld_c")
        ld_taps = sem("ld_taps")
        ld_state = sem("ld_state")
        ld_bup = sem("ld_bup")
        bup_clear = sem("bup_clear")
        sel_ready = sem("sel_ready")
        ld_late = sem("ld_late")
        ld_bdown = sem("ld_bdown")
        landed = [sem(f"landed{i}") for i in range(RING)]
        chunk_used = sem("chunk_used")
        consts = sem("consts")
        zeroed = sem("zeroed")
        silu_c = sem("silu_c")
        turned = sem("turned")
        turn_out = sem("turn_out")
        sq1 = sem("sq1")
        stat1 = sem("stat1")
        rms1 = sem("rms1")
        h1 = sem("h1")
        z_done = sem("z_done")
        z_out = sem("z_out")
        u_ready = sem("u_ready")
        uf_ready = sem("uf_ready")
        vs_conv = sem("vs_conv")
        v_ready = sem("v_ready")
        st_turned = sem("st_turned")
        st_out = sem("st_out")
        pool_step = sem("pool_step")
        pooled = sem("pooled")
        mean_done = sem("mean_done")
        centred = sem("centred")
        vsq = sem("vsq")
        var_done = sem("var_done")
        vrms = sem("vrms")
        ln_ready = sem("ln_ready")
        ln_sig = sem("ln_sig")
        vact = sem("vact")
        yp_done = sem("yp_done")
        yp_out = sem("yp_out")
        yc_done = sem("yc_done")
        m_ready = sem("m_ready")
        yo_done = sem("yo_done")
        x2_out = sem("x2_out")
        sq2 = sem("sq2")
        stat2 = sem("stat2")
        rms2 = sem("rms2")
        h2 = sem("h2")
        logits = sem("logits")
        h2_turned = sem("h2_turned")
        h2_out = sem("h2_out")
        shifted = sem("shifted")
        expd = sem("expd")
        mask_ready = sem("mask_ready")
        wgt_ready = sem("wgt_ready")
        ranked = sem("ranked")
        rank_ready = sem("rank_ready")
        wT_turned = sem("wT_turned")
        wT_out = sem("wT_out")
        bd_done = sem("bd_done")
        bd_out = sem("bd_out")
        turn_clear = sem("turn_clear")
        pass_ready = sem("pass_ready")
        hot_ready = sem("hot_ready")
        hotw_ready = sem("hotw_ready")
        gathered = sem("gathered")
        hg_out = sem("hg_out")
        glu_out = sem("glu_out")
        sig_out = sem("sig_out")
        lin_clip = sem("lin_clip")
        gs_out = sem("gs_out")
        o_ready = sem("o_ready")
        y_out = sem("y_out")
        o_turned = sem("o_turned")
        oT_out = sem("oT_out")
        combined = sem("combined")
        added = sem("added")
        comb_turned = sem("comb_turned")
        comb_out = sem("comb_out")
        x3_out = sem("x3_out")
        sq3 = sem("sq3")
        stat3 = sem("stat3")
        rms3 = sem("rms3")
        yn = sem("yn")
        fin_turned = sem("fin_turned")
        fin_out = sem("fin_out")
        st_sent = sem("st_sent")
        old_sent = sem("old_sent")
        y_sent = sem("y_sent")
        dve_done = sem("dve_done")
        pool_done = sem("pool_done")

        UP_BANKS = (0, 1, 2, 0, 1, 2)
        HG_BANK = 3
        T_BANK = 5
        BD_BANKS = (0, 1, 2, 7)
        SUM_ORDER = (0, 2, 1, 3, 4, 6, 5, 7)
        GAT = NE + 1

        block = ctx.enter_context(nc.Block())

        @block.sync
        def _(sp):
            def source(kind, i):
                cols = slice(i * COLS, (i + 1) * COLS)
                if kind == "conv_out":
                    return w_conv_out[0].rearrange("(k p) n -> p k n", p=P)
                w = {"ada": w_ada, "in": w_in, "out": w_out}[kind]
                return w[0].rearrange("(k p) n -> p k n", p=P)[:, :, cols]

            for c, (kind, i) in enumerate(MIXER_CHUNKS):
                if c >= RING:
                    sp.wait_ge(chunk_used, c - RING + 1)
                src = source(kind, i)
                dst = ring[:, c % RING, :].rearrange("p (k n) -> p k n", k=src.shape[1])
                sp.dma_start(dst, src).then_inc(landed[c % RING], 16)

            up = w_up[0].rearrange("e (k p) n -> e p k n", p=P)
            down = w_down[0].rearrange("e (k p) n -> e p k n", p=P)

            def expert_weights(n, e):
                for j, (w, col) in enumerate(((up, 0), (up, D), (up, COLS), (up, D + COLS),
                                              (down, 0), (down, COLS))):
                    c = NMIX + j
                    sp.wait_ge(chunk_used, n * EXPERT_CHUNKS + (c - RING + 1))
                    dst = ring[:, c % RING, :].rearrange("p (k n) -> p k n", k=KT)
                    sp.dma_start(dst, w[e, :, :, col:col + COLS]).then_inc(landed[c % RING], 16)

            with sp.Fori(0, NE) as e:
                expert_weights(e, e)
            sp.wait_ge(rank_ready, 1)
            most = sp.value_load(cnti[0:1, NE + 2:NE + 3], min_val=0, max_val=NT)
            with sp.If(most > SLOTS):
                with sp.Fori(1, PASSES) as p:
                    with sp.Fori(0, NE) as e:
                        expert_weights(p * NE + e, e)

            sp.wait_ge(fin_out, 2)
            sp.dma_start(y_prompt[0, 0:P, :], rows[:, 0, :]).then_inc(y_sent, 16)
            sp.wait_ge(fin_out, 4)
            sp.dma_start(y_prompt[0, P:2 * P, :], rows[:, 1, :]).then_inc(y_sent, 16)
            sp.wait_ge(fin_out, 6)
            sp.dma_start(y_sample.rearrange("b t d -> (b t) d"), rows[0:DEC, 2, :]).then_inc(y_sent, 16)
            sp.wait_ge(y_sent, 3 * 16)
            sp.wait_ge(st_sent, 16 * (2 + 2 * DEC_B))

        @block.gpsimd
        def _(pool):
            pool.memset(ident[:, :], 0.0).then_inc(zeroed, 1)
            pool.memset(upper[:, :], 0.0).then_inc(zeroed, 1)
            pool.memset(ones[:, :], 1.0).then_inc(consts, 1)
            pool.memset(avg[:, 0, :], 1.0 / D).then_inc(consts, 1)
            pool.memset(avg[:, 1, :], 1.0 / DC).then_inc(consts, 1)
            pool.memset(epsc[:, :], EPS).then_inc(consts, 1)
            pool.wait_ge(zeroed, 2)
            pool.affine_select(out=ident[:, :], in_=ident[:, :], compare_op=ALU.not_equal, fill=1.0,
                               base=0, pattern=[[-1, P]], channel_multiplier=1).then_inc(consts, 1)
            pool.affine_select(out=upper[:, :], in_=upper[:, :], compare_op=ALU.is_ge, fill=1.0,
                               base=0, pattern=[[-1, P]], channel_multiplier=1).then_inc(consts, 1)
            pool.dma_start(new_conv_sample[0, :, 0:CBUF - DEC_T, :],
                           state_conv[0, :, DEC_T:CBUF, :]).then_inc(old_sent, 16)
            pool.dma_start(new_pool_sample[0, :, 0:PBUF - DEC_T, :],
                           state_pool[0, :, DEC_T:PBUF, :]).then_inc(old_sent, 16)
            pool.iota(iota[:, :], pattern=[[1, SLOTS]], base=0, channel_multiplier=0,
                      allow_small_or_imprecise_dtypes=True).then_inc(consts, 1)
            pool.iota(icnt[:, :, :], pattern=[[0, CT_], [1, 16]], base=1, channel_multiplier=0,
                      allow_small_or_imprecise_dtypes=True).then_inc(pool_done, 1)
            pool.wait_ge(pool_done, 1)
            for g, w in enumerate(WINDOWS):
                pool.tensor_scalar(icnt[:, g, :], icnt[:, g, :], float(w), None, ALU.min)\
                    .then_inc(consts, 1)
            (f_p, f_s), (a_p, a_s), (b_p, b_s) = pool_bufs
            pool.memset(f_p[:, :, 0:PBUF], 0.0).then_inc(pool_step, 1)
            pool.wait_ge(z_out, 3 * CT_)
            pool.wait_ge(turn_out, 16)
            pool.tensor_copy(f_p[:, :, PBUF:PBUF + SEQ], upT[:, :, 0:SEQ]).then_inc(pool_step, 1)
            for g in range(CT_):
                pool.tensor_copy(f_s[:, g, :, PBUF:PBUF + DEC_T],
                                 upT[:, g, SEQ:NT].rearrange("p (s t) -> p s t", t=DEC_T))\
                    .then_inc(pool_step, 1)
            pool.wait_ge(pool_step, 2 + CT_)
            src, dst = (f_p, f_s), (a_p, a_s)
            for g, w in enumerate(WINDOWS):
                lag, first = w // 2, w - 1
                pool.tensor_tensor(dst[0][:, g:, first:], src[0][:, g:, first:],
                                   src[0][:, g:, first - lag:PBUF + SEQ - lag], ALU.add)\
                    .then_inc(pool_step, 1)
                for q in range(g, CT_):
                    pool.tensor_tensor(dst[1][:, q, :, first:], src[1][:, q, :, first:],
                                       src[1][:, q, :, first - lag:PBUF + DEC_T - lag], ALU.add)\
                        .then_inc(pool_step, 1)
                pool.wait_ge(pool_step, 2 + CT_ + (g + 1) + sum(CT_ - q for q in range(g + 1)))
                src, dst = dst, ((b_p, b_s) if g % 2 == 0 else (a_p, a_s))

            pool.wait_ge(old_sent, 32)
            pool.wait_ge(yp_done, KT)
            pool.dma_start(bdown, b_down[0]).then_inc(ld_bdown, 16)
            pool.wait_ge(h2_turned, 2 * NJ)
            pool.memset(bup, 0.0).then_inc(bup_clear, 1)
            pool.wait_ge(bup_clear, 1)
            pool.dma_start(bup[0:NE, :], b_up[0]).then_inc(ld_bup, 16)

        @block.scalar
        def _(act):
            act.dma_start(rows[:, 0:2, :], x_prompt[0].rearrange("(j p) d -> p j d", p=P)).then_inc(ld_x, 16)
            act.dma_start(rows[0:DEC, 2, :], x_sample.rearrange("b t d -> (b t) d")).then_inc(ld_x, 16)
            act.dma_start(c_rows[0:1, :], c_prompt).then_inc(ld_c, 16)
            act.dma_start(c_rows[1:SEQS, :], c_sample).then_inc(ld_c, 16)
            for name, ap in (("b_ada", b_ada[0]), ("b_in", b_in[0]), ("norm_mix", norm_mix[0]),
                             ("norm_ffn", norm_ffn[0]), ("norm_final", norm_final),
                             ("pool_scale", pool_scale[0]), ("conv_b", conv_b[0]),
                             ("conv_ln_g", conv_ln_g[0]), ("conv_ln_b", conv_ln_b[0])):
                a, n = VEC_ROWS[name]
                act.dma_start(vec_rows[a:a + n, :], ap.rearrange("(r p) -> r p", p=P)).then_inc(ld_vec, 16)
            act.dma_start(tap_rows[:, :], conv_w[0]).then_inc(ld_taps, 16)
            act.dma_start(sconv_rows, state_conv[0].rearrange("s t d -> (s t) d")
                          .rearrange("(j p) d -> p j d", j=2)).then_inc(ld_state, 16)
            act.dma_start(spool_rows, state_pool[0].rearrange("s t d -> (s t) d")).then_inc(ld_state, 16)
            act.dma_start(wpool[:, :, :], w_pool[0].rearrange("g p n -> p g n")).then_inc(ld_late, 16)
            act.dma_start(wrouter[:, :, :], w_router[0].rearrange("(k p) n -> p k n", p=P)).then_inc(ld_late, 16)
            act.dma_start(brout[:, :], b_router.broadcast_to([P, NE])).then_inc(ld_late, 16)

            act.wait_ge(ld_c, 32)
            act.activation(sq[0:SEQS, 0:4, 0:256], c_rows.rearrange("p (k n) -> p k n", k=4),
                           ACT.Sigmoid).then_inc(silu_c, 1)

            for k in range(KT):
                act.wait_ge(turn_out, k + 2)
                if k == 0:
                    act.wait_ge(silu_c, 2)
                act.activation(sq[:, k, :], xT[:, k, :], ACT.Square).then_inc(sq1, 1)
            act.wait_ge(stat1, 1)
            act.wait_ge(consts, 4)
            act.activation(rms[:, :], ps[:, 1, 0:NT], ACT.Sqrt, bias=epsc[:, :]).then_inc(rms1, 1)

            for t in range(28):
                act.wait_ge(z_done, t + 1)
                src, bias = ps[:, t % 8, 0:NT], vcol("b_in", t)
                if t < CT_:
                    act.activation(uT[:, t, :], src, ACT.Identity, bias=bias).then_inc(z_out, 1)
                elif t < 2 * CT_:
                    act.activation(gateT[:, t - CT_, :], src, ACT.Sigmoid, bias=bias).then_inc(z_out, 1)
                elif t < 3 * CT_:
                    act.activation(upT[:, t - 2 * CT_, :], src, ACT.Identity, bias=bias).then_inc(z_out, 1)
                else:
                    act.activation(sgT[:, t - 3 * CT_, :], src, ACT.Sigmoid, bias=bias).then_inc(z_out, 1)

            for i in range(4):
                n = (CBUF, DEC, PBUF, DEC)[i]
                act.wait_ge(st_turned, i + 1)
                act.copy(stage[0:n, i * DC:(i + 1) * DC], ps[0:n, i, :]).then_inc(st_out, 1)
            act.wait_ge(st_out, 4)
            act.dma_start(new_conv_prompt[0, 0], stage[0:CBUF, 0:DC]).then_inc(st_sent, 16)
            act.dma_start(new_pool_prompt[0, 0], stage[0:PBUF, 2 * DC:3 * DC]).then_inc(st_sent, 16)
            for s in range(DEC_B):
                act.dma_start(new_conv_sample[0, s, CBUF - DEC_T:CBUF, :],
                              stage[s * DEC_T:(s + 1) * DEC_T, DC:2 * DC]).then_inc(st_sent, 16)
                act.dma_start(new_pool_sample[0, s, PBUF - DEC_T:PBUF, :],
                              stage[s * DEC_T:(s + 1) * DEC_T, 3 * DC:4 * DC]).then_inc(st_sent, 16)

            act.wait_ge(centred, 1)
            act.activation(gateT, vT, ACT.Square).then_inc(vsq, 1)
            act.wait_ge(var_done, 1)
            act.activation(rms[:, :], ps[:, 5, 0:NT], ACT.Sqrt, bias=epsc[:, :]).then_inc(vrms, 1)
            for c in range(CT_):
                act.wait_ge(ln_ready, c + 1)
                act.activation(gateT[:, c, :], vT[:, c, :], ACT.Sigmoid).then_inc(ln_sig, 1)

            for k in range(KT):
                act.wait_ge(x2_out, k + 1)
                act.activation(sq[:, k, :], xT[:, k, :], ACT.Square).then_inc(sq2, 1)
            act.wait_ge(stat2, 1)
            act.activation(rms[:, :], ps[:, 4, 0:NT], ACT.Sqrt, bias=epsc[:, :]).then_inc(rms2, 1)

            act.wait_ge(st_sent, 16 * (2 + 2 * DEC_B))
            for j, (_, n) in enumerate(TOK_TILES):
                for half in range(2):
                    i = 2 * j + half
                    act.wait_ge(h2_turned, i + 1)
                    act.copy(rows[0:n, j, half * BANK:(half + 1) * BANK],
                             ps[0:n, (0, 1, 2, 3, 4, 7)[i], :]).then_inc(h2_out, 1)
            act.wait_ge(shifted, 1)
            act.activation(wgt[:, :, :], lg[:, :, :], ACT.Exp).then_inc(expd, 1)
            for t in range(KT):
                act.wait_ge(bd_done, t + 1)
                act.copy(accT[:, t, :], ps[:, BD_BANKS[t % 4], 0:NT]).then_inc(bd_out, 1)

            def gather_out(g):
                act.wait_ge(gathered, g)
                act.copy(hgT, ps[:, HG_BANK:HG_BANK + 2, :]
                         .rearrange("p b (k s) -> p (b k) s", s=SLOTS)).then_inc(hg_out, 1)

            def expert_pass(n0, p):
                gather_out(p * GAT + 1)
                with act.Fori(0, NE) as e:
                    n = n0 + e
                    for h in range(2):
                        act.wait_ge(glu_out, 2 * n + h + 1)
                        act.activation(sig[:, h, :], glu[:, h, :], ACT.Sigmoid, scale=ALPHA)\
                            .then_inc(sig_out, 1)
                    gather_out(p * GAT + e + 2)
                    for h in range(2):
                        act.wait_ge(o_turned, 2 * n + h + 1)
                        act.copy(oT[:, h, :], ps[:, T_BANK + h, :]).then_inc(oT_out, 1)
                    for h in range(2):
                        act.wait_ge(chunk_used, NMIX + n * EXPERT_CHUNKS + 5 + h)
                        act.copy(yrow[:, h * BANK:(h + 1) * BANK], ps[:, UP_BANKS[4 + h], :])\
                            .then_inc(y_out, 1)

            expert_pass(0, 0)
            most = act.value_load(cnti[0:1, NE + 2:NE + 3], min_val=0, max_val=NT)
            with act.If(most > SLOTS):
                with act.Fori(1, PASSES) as p:
                    expert_pass(p * NE, p)

            for k in range(KT):
                act.wait_ge(x3_out, k + 1)
                act.activation(sq[:, k, :], xT[:, k, :], ACT.Square).then_inc(sq3, 1)
            act.wait_ge(stat3, 1)
            act.activation(rms[:, :], ps[:, 0, 0:NT], ACT.Sqrt, bias=epsc[:, :]).then_inc(rms3, 1)
            for j, (_, n) in enumerate(TOK_TILES):
                for half in range(2):
                    i = 2 * j + half
                    act.wait_ge(fin_turned, i + 1)
                    act.copy(rows[0:n, j, half * BANK:(half + 1) * BANK], ps[0:n, 1 + i, :])\
                        .then_inc(fin_out, 1)

        @block.vector
        def _(dve):
            step = [0]

            def link(ins):
                step[0] += 1
                ins.then_inc(dve_done, 1)
                dve.wait_ge(dve_done, step[0])

            V = nc.vector
            V.memset(uf_p[:, :, 0:CBUF], 0.0).then_inc(dve_done, 1)
            V.memset(rankm[:, :, NE:NE + 1], -1.0).then_inc(dve_done, 1)
            V.memset(cntf[:, :], 0.0).then_inc(dve_done, 1)
            step[0] = 3

            for g in range(16):
                dve.wait_ge(turned, g + 1)
                bank = ps[:, g % 8, :]
                if g == 0:
                    ins = V.tensor_copy(vec[:, 0:NVEC], bank[:, 0:NVEC])
                elif g < 9:
                    ins = V.tensor_copy(xT[:, g - 1, :], bank[:, 0:NT])
                elif g == 9:
                    ins = V.tensor_copy(silc[:, :, :], bank[:, 0:KT * SEQS].rearrange("p (k s) -> p k s", k=KT))
                elif g == 10:
                    ins = V.tensor_copy(taps[:, :, :], bank[:, 0:CT_ * TAPS].rearrange("p (c w) -> p c w", c=CT_))
                elif g < 15:
                    ins = V.tensor_copy(uf_s[:, g - 11, :, 0:CBUF],
                                        bank[:, 0:DEC_B * CBUF].rearrange("p (s t) -> p s t", t=CBUF))
                else:
                    for c in range(CT_):
                        ins = V.tensor_copy(pool_bufs[0][1][:, c, :, 0:PBUF],
                                            bank[:, c * 120:(c + 1) * 120].rearrange("p (s t) -> p s t", t=PBUF))
                ins.then_inc(turn_out, 1)
                if g == 0:
                    dve.wait_ge(silu_c, 1)
                    V.tensor_tensor(c_rows.rearrange("p (k n) -> p k n", k=4),
                                    c_rows.rearrange("p (k n) -> p k n", k=4),
                                    sq[0:SEQS, 0:4, 0:256], ALU.mult).then_inc(silu_c, 1)

            dve.wait_ge(consts, 11)
            link(V.reciprocal(icnt[:, :, :], icnt[:, :, :]))

            def mod_out(first, last, bank, at):
                a = VEC_ROWS["b_ada"][0]
                n = last - first
                link(V.tensor_tensor(modT[:, first:last, :],
                                     ps[:, bank, at:at + n * SEQS].rearrange("p (k s) -> p k s", s=SEQS),
                                     vec[:, a + first:a + last].unsqueeze(2).to_broadcast([P, n, SEQS]), ALU.add))

            def gain(sc, norm):
                part = modT[:, sc * KT:(sc + 1) * KT, :]
                link(V.tensor_scalar(part, part, 1.0, None, ALU.add))
                link(V.tensor_tensor(part, part, vcols(norm).unsqueeze(2).to_broadcast([P, KT, SEQS]), ALU.mult))

            def per_seq(i):
                return modT[:, i * KT:(i + 1) * KT, 1:SEQS].unsqueeze(3).to_broadcast([P, KT, DEC_B, DEC_T])

            def modulate(sh, sc, ready):
                link(V.reciprocal(rstd[:, :], rms[:, :]))
                link(V.tensor_tensor(hT[:, :, :], xT[:, :, :],
                                     rstd[:, :].unsqueeze(1).to_broadcast([P, KT, NT]), ALU.mult))
                link(V.tensor_tensor(decoded(hT), decoded(hT), per_seq(sc), ALU.mult))
                link(V.tensor_tensor(decoded(hT), decoded(hT), per_seq(sh), ALU.add))
                for k in range(KT):
                    V.tensor_scalar(hT[:, k, 0:SEQ], hT[:, k, 0:SEQ], modT[:, sc * KT + k, 0:1],
                                    modT[:, sh * KT + k, 0:1], ALU.mult, ALU.add).then_inc(ready, 1)

            dve.wait_ge(turn_out, 16)
            dve.wait_ge(chunk_used, 4)
            mod_out(0, 2 * KT, 2, 0)
            gain(1, "norm_mix")
            dve.wait_ge(rms1, 1)
            modulate(0, 1, h1)

            for c in range(CT_):
                dve.wait_ge(z_out, CT_ + c + 1)
                V.tensor_tensor(uT[:, c, :], uT[:, c, :], gateT[:, c, :], ALU.mult).then_inc(u_ready, 1)
            for c in range(CT_):
                dve.wait_ge(u_ready, c + 1)
                V.tensor_copy(uf_p[:, c, CBUF:CBUF + SEQ], uT[:, c, 0:SEQ]).then_inc(uf_ready, 1)
                V.tensor_copy(uf_s[:, c, :, CBUF:CBUF + DEC_T],
                              uT[:, c, SEQ:NT].rearrange("p (s t) -> p s t", t=DEC_T)).then_inc(uf_ready, 1)
            dve.wait_ge(uf_ready, 2 * CT_)
            for w in range(TAPS):
                for c in range(CT_):
                    for q, (out, hist) in enumerate((
                            (vT[:, c, 0:SEQ], uf_p[:, c, w:w + SEQ]),
                            (vT[:, c, SEQ:NT].rearrange("p (s t) -> p s t", t=DEC_T),
                             uf_s[:, c, :, w:w + DEC_T]))):
                        tap = taps[:, c, w:w + 1]
                        if w == 0:
                            V.tensor_scalar(out, hist, tap, vcol("conv_b", c), ALU.mult, ALU.add)\
                                .then_inc(v_ready, 1)
                        else:
                            dve.wait_ge(v_ready, 2 * CT_ * (w - 1) + 2 * c + q + 1)
                            V.scalar_tensor_tensor(out=out, in0=hist, scalar=tap, in1=out,
                                                   op0=ALU.mult, op1=ALU.add).then_inc(v_ready, 1)

            dve.wait_ge(pool_step, 2 + 2 * CT_ + 10)
            dve.wait_ge(st_turned, 4)
            for g, w in enumerate(WINDOWS):
                s_p, s_s = pool_bufs[1 + g % 2]
                early = s_p[:, g, PBUF:PBUF + 16]
                V.tensor_tensor(early, early, icnt[:, g, :], ALU.mult).then_inc(pooled, 1)
                V.scalar_tensor_tensor(out=upT[:, g, 16:SEQ], in0=s_p[:, g, PBUF + 16:PBUF + SEQ],
                                       scalar=1.0 / w, in1=upT[:, g, 16:SEQ],
                                       op0=ALU.mult, op1=ALU.subtract).then_inc(pooled, 1)
                dec = upT[:, g, SEQ:NT].rearrange("p (s t) -> p s t", t=DEC_T)
                V.scalar_tensor_tensor(out=dec, in0=s_s[:, g, :, PBUF:PBUF + DEC_T], scalar=1.0 / w,
                                       in1=dec, op0=ALU.mult, op1=ALU.subtract).then_inc(pooled, 1)
                dve.wait_ge(pooled, 4 * g + 1)
                V.tensor_tensor(upT[:, g, 0:16], early, upT[:, g, 0:16], ALU.subtract).then_inc(pooled, 1)

            dve.wait_ge(v_ready, 2 * CT_ * TAPS)
            dve.wait_ge(mean_done, 1)
            V.tensor_tensor(vT, vT, ps[:, 4, 0:NT].unsqueeze(1).to_broadcast([P, CT_, NT]), ALU.subtract)\
                .then_inc(centred, 1)
            dve.wait_ge(vrms, 1)
            link(V.reciprocal(rstd[:, :], rms[:, :]))
            dve.wait_ge(centred, 1)
            link(V.tensor_tensor(vT, vT, rstd[:, :].unsqueeze(1).to_broadcast([P, CT_, NT]), ALU.mult))
            for c in range(CT_):
                V.tensor_scalar(vT[:, c, :], vT[:, c, :], vcol("conv_ln_g", c), vcol("conv_ln_b", c),
                                ALU.mult, ALU.add).then_inc(ln_ready, 1)
            for c in range(CT_):
                dve.wait_ge(ln_sig, c + 1)
                V.tensor_tensor(vT[:, c, :], vT[:, c, :], gateT[:, c, :], ALU.mult).then_inc(vact, 1)

            dve.wait_ge(z_out, 28)
            for t in range(KT):
                dve.wait_ge(yp_done, t + 1)
                V.scalar_tensor_tensor(out=sgT[:, KT + t, :], in0=ps[:, t % 4, 0:NT],
                                       scalar=vcol("pool_scale", t), in1=sgT[:, KT + t, :],
                                       op0=ALU.mult, op1=ALU.mult).then_inc(yp_out, 1)
            dve.wait_ge(chunk_used, MIX_AT["ada", 5] + 1)
            mod_out(2 * KT, 3 * KT, 6, 0)
            for t in range(KT):
                dve.wait_ge(yc_done, t + 1)
                link(V.tensor_tensor(sgT[:, t, :], ps[:, t % 4, 0:NT], sgT[:, t, :], ALU.mult))
                V.tensor_tensor(hT[:, t, :], sgT[:, t, :], sgT[:, KT + t, :], ALU.add).then_inc(m_ready, 1)
            def residual(t, y, gt, done):
                link(V.tensor_tensor(y[1], y[1], modT[:, gt * KT + t, 1:SEQS].unsqueeze(2)
                                     .to_broadcast([P, DEC_B, DEC_T]), ALU.mult) if y[2] is None else
                     V.tensor_tensor(y[2], y[1], modT[:, gt * KT + t, 1:SEQS].unsqueeze(2)
                                     .to_broadcast([P, DEC_B, DEC_T]), ALU.mult))
                V.scalar_tensor_tensor(out=xT[:, t, 0:SEQ], in0=y[0], scalar=modT[:, gt * KT + t, 0:1],
                                       in1=xT[:, t, 0:SEQ], op0=ALU.mult, op1=ALU.add)
                xs = xT[:, t, SEQ:NT].rearrange("p (s t) -> p s t", t=DEC_T)
                V.tensor_tensor(xs, xs, y[1] if y[2] is None else y[2], ALU.add).then_inc(done, 1)

            for t in range(KT):
                dve.wait_ge(yo_done, t + 1)
                tmp = rstd[:, t * DEC:(t + 1) * DEC].rearrange("p (s t) -> p s t", t=DEC_T)
                residual(t, (ps[:, t % 4, 0:SEQ],
                             ps[:, t % 4, SEQ:NT].rearrange("p (s t) -> p s t", t=DEC_T), tmp), 2, x2_out)
            dve.wait_ge(chunk_used, MIX_AT["ada", 9] + 1)
            mod_out(3 * KT, 5 * KT, 7, 0)
            gain(4, "norm_ffn")
            dve.wait_ge(rms2, 1)
            dve.wait_ge(x2_out, KT)
            modulate(3, 4, h2)
            dve.wait_ge(chunk_used, NMIX)
            mod_out(5 * KT, 6 * KT, 6, 0)

            link(V.memset(lg[:, :, :], 0.0))
            dve.wait_ge(logits, 1)
            dve.wait_ge(ld_late, 48)
            for j, (_, n) in enumerate(TOK_TILES):
                ins = V.tensor_tensor(lg[0:n, j, :], ps[0:n, 5, j * NE:(j + 1) * NE], brout[0:n, :], ALU.add)
            link(ins)
            for j in range(NJ):
                ins = V.max(out=top8[:, j, :], in_=lg[:, j, :])
            link(ins)
            fourth = top8[:, :, TOPK - 1:TOPK].to_broadcast([P, NJ, NE])
            V.tensor_tensor(mask[:, :, :], lg[:, :, :], fourth, ALU.is_gt)
            link(V.tensor_tensor(eq[:, :, :], lg[:, :, :], fourth, ALU.is_equal))
            V.tensor_tensor(lg[:, :, :], lg[:, :, :], top8[:, :, 0:1].to_broadcast([P, NJ, NE]),
                            ALU.subtract).then_inc(shifted, 1)
            V.tensor_reduce(need[:, :], mask[:, :, :], AX.X, ALU.add)
            onesv = ones[:, 0:NE]
            for j in range(NJ):
                ins = V.tensor_tensor_scan(cum[:, j, :], onesv, eq[:, j, :], 0.0, ALU.mult, ALU.add)
            link(ins)
            link(V.tensor_tensor(cum[:, :, :], cum[:, :, :], need[:, :].unsqueeze(2)
                                 .to_broadcast([P, NJ, NE]), ALU.add))
            link(V.scalar_tensor_tensor(out=eq[:, :, :], in0=cum[:, :, :], scalar=float(TOPK) + 0.5,
                                        in1=eq[:, :, :], op0=ALU.is_lt, op1=ALU.mult))
            link(V.tensor_tensor(mask[:, :, :], mask[:, :, :], eq[:, :, :], ALU.add))
            V.memset(mask[DEC:2 * DEC, NJ - 1, :], 0.0)
            V.memset(mask[2 * DEC:P, NJ - 1, :], 0.0).then_inc(mask_ready, 1)
            dve.wait_ge(mask_ready, 1)
            dve.wait_ge(expd, 1)
            link(V.tensor_tensor(wgt[:, :, :], wgt[:, :, :], mask[:, :, :], ALU.mult))
            link(V.tensor_reduce(need[:, :], wgt[:, :, :], AX.X, ALU.add))
            link(V.tensor_scalar(need[:, :], need[:, :], 1e-30, None, ALU.max))
            link(V.reciprocal(need[:, :], need[:, :]))
            V.tensor_tensor(wgt[:, :, :], wgt[:, :, :], need[:, :].unsqueeze(2)
                            .to_broadcast([P, NJ, NE]), ALU.mult).then_inc(wgt_ready, 1)
            dve.wait_ge(ranked, 1)
            rk = ps[:, 6, 0:NJ * NE].rearrange("p (j e) -> p j e", e=NE)
            link(V.scalar_tensor_tensor(out=eq[:, :, :], in0=rk, scalar=1.0, in1=mask[:, :, :],
                                        op0=ALU.add, op1=ALU.mult))
            link(V.tensor_scalar(rankm[:, :, 0:NE], eq[:, :, :], -1.0, None, ALU.add))
            link(V.tensor_copy(cntf[:, 1:NE + 1], ps[0:1, 6, NJ * NE:(NJ + 1) * NE]))
            link(V.tensor_reduce(cntf[:, NE + 2:NE + 3], cntf[:, 1:NE + 1], AX.X, ALU.max))
            V.tensor_copy(cnti[:, :], cntf[:, :]).then_inc(rank_ready, 1)
            counts = ps[:, 6, NJ * NE:(NJ + 1) * NE]
            link(V.tensor_scalar(starts[:, 1, :], counts, WIDTHS[0] + 0.5, float(QW), ALU.is_gt, ALU.mult))
            link(V.tensor_scalar(starts[:, 2, :], counts, WIDTHS[1] + 0.5, float(2 * QW), ALU.is_gt, ALU.mult))
            link(V.tensor_tensor(starts[:, 3, :], starts[:, 1, :], starts[:, 2, :], ALU.add))
            V.memset(rtab[:, :, :, NE:NE + 1], -1.0)
            V.tensor_copy(rtab[:, 0, :, 0:NE], rankm[:, :, 0:NE])
            for q in range(1, NQ):
                ins = V.tensor_tensor(rtab[:, q, :, 0:NE], rankm[:, :, 0:NE],
                                      starts[:, q, :].unsqueeze(1).to_broadcast([P, NJ, NE]), ALU.subtract)
            link(ins)
            dve.wait_ge(wT_turned, 1)
            V.tensor_copy(wT[:, :], ps[0:NE, 5, 0:NT]).then_inc(wT_out, 1)
            dve.wait_ge(wT_out, 1)
            V.memset(ps[:, T_BANK:T_BANK + 2, :], 0.0).then_inc(turn_clear, 1)
            dve.wait_ge(bd_out, KT)
            V.memset(ps[:, 0:3, :], 0.0).then_inc(added, 1)
            V.memset(yrow, 0.0).then_inc(y_out, 1)

            def hot_for(e):
                for j in range(NJ):
                    ins = V.tensor_scalar(hot[:, j, :], iota[:, :], rankm[:, j, bass.ds(e, 1)], None,
                                          ALU.is_equal)
                ins.then_inc(hot_ready, 1)

            def sel_for(e):
                V.tensor_scalar(sel[:, :], ones[:, :], ident[:, bass.ds(e, 1)], None, ALU.mult)\
                    .then_inc(sel_ready, 1)

            def expert_pass(n0, p):
                dve.wait_ge(pass_ready, p + 1)
                hot_for(0)
                sel_for(0)
                V.memset(comb, 0.0).then_inc(comb_out, 1)
                with dve.Fori(0, NE) as e:
                    n = n0 + e
                    dve.wait_ge(gathered, p * GAT + e + 1)
                    hot_for(e + 1)
                    for j in range(NJ):
                        for q in range(NQ):
                            ins = V.tensor_scalar(hotw[:, j, q * QW:(q + 1) * QW], iota[:, 0:QW],
                                                  rtab[:, q, j, bass.ds(e, 1)],
                                                  wgt[:, j, bass.ds(e, 1)], ALU.is_equal, ALU.mult)
                    ins.then_inc(hotw_ready, 1)
                    for h in range(2):
                        dve.wait_ge(chunk_used, NMIX + n * EXPERT_CHUNKS + 2 * h + 1)
                        V.tensor_scalar(glu[:, h, :], ps[:, UP_BANKS[2 * h], :], LIMIT, None, ALU.min)\
                            .then_inc(glu_out, 1)
                        dve.wait_ge(chunk_used, NMIX + n * EXPERT_CHUNKS + 2 * h + 2)
                        V.tensor_scalar(lin[:, h, :], ps[:, UP_BANKS[2 * h + 1], :], LIMIT, -LIMIT,
                                        ALU.min, ALU.max).then_inc(lin_clip, 1)
                        dve.wait_ge(sig_out, 2 * n + h + 1)
                        dve.wait_ge(glu_out, 2 * n + h + 1)
                        V.tensor_tensor(glu[:, h, :], glu[:, h, :], sig[:, h, :], ALU.mult)\
                            .then_inc(gs_out, 1)
                        dve.wait_ge(lin_clip, 2 * n + h + 1)
                        dve.wait_ge(gs_out, 2 * n + h + 1)
                        V.scalar_tensor_tensor(out=otok[:, h, :], in0=lin[:, h, :], scalar=1.0,
                                               in1=glu[:, h, :], op0=ALU.add, op1=ALU.mult)\
                            .then_inc(o_ready, 1)
                    sel_for(e + 1)
                    add_results(p * GAT + e)
                    dve.wait_ge(comb_turned, n + 1)
                    V.tensor_copy(comb, ps[:, T_BANK + 2, 0:NT]).then_inc(comb_out, 1)
                add_results(p * GAT + NE)

            def add_results(r):
                for i, k in enumerate(SUM_ORDER):
                    dve.wait_ge(combined, KT * r + i + 1)
                    dve.wait_ge(added, KT * r + 1)
                    V.tensor_tensor(accT[:, k, :], accT[:, k, :], ps[:, T_BANK + i % 3, 0:NT], ALU.add)\
                        .then_inc(added, 1)

            V.memset(need[:, :], 0.0).then_inc(pass_ready, 1)
            expert_pass(0, 0)
            dve.wait_ge(added, KT * GAT + 1)
            most = dve.value_load(cnti[0:1, NE + 2:NE + 3], min_val=0, max_val=NT)
            with dve.If(most > SLOTS):
                with dve.Fori(1, PASSES) as p:
                    dve.wait_ge(hotw_ready, p * NE)
                    dve.wait_ge(hot_ready, p * GAT)
                    V.tensor_scalar(rankm[:, :, :], rankm[:, :, :], float(-SLOTS), None, ALU.add)\
                        .then_inc(rank_ready, 1)
                    dve.wait_ge(rank_ready, p + 1)
                    for q in range(NQ):
                        ins = V.tensor_scalar(rtab[:, q, :, :], rankm[:, :, :], float(-q * QW), None, ALU.add)
                    ins.then_inc(pass_ready, 1)
                    expert_pass(p * NE, p)
                    dve.wait_ge(added, (p + 1) * (KT * GAT) + 1)

            for t in range(KT):
                residual(t, (accT[:, t, 0:SEQ],
                             accT[:, t, SEQ:NT].rearrange("p (s t) -> p s t", t=DEC_T), None), 5, x3_out)
            dve.wait_ge(rms3, 1)
            link(V.reciprocal(rstd[:, :], rms[:, :]))
            dve.wait_ge(x3_out, KT)
            for t in range(KT):
                V.scalar_tensor_tensor(out=hT[:, t, :], in0=xT[:, t, :], scalar=vcol("norm_final", t),
                                       in1=rstd[:, :], op0=ALU.mult, op1=ALU.mult).then_inc(yn, 1)

        @block.tensor
        def _(pe):
            def chunk(c, k):
                return ring[:, c % RING, :].rearrange("p (k n) -> p k n", k=k)

            def chunk_landed(c):
                pe.wait_ge(landed[c % RING], 16 * (c // RING + 1))

            pe.wait_ge(consts, 6)
            for g in range(16):
                bank = ps[:, g % 8, :]
                if g >= 8:
                    pe.wait_ge(turn_out, g - 7)
                if g == 0:
                    pe.wait_ge(ld_vec, 16 * len(VEC_ROWS))
                    ins = pe.transpose(bank[:, 0:NVEC], vec_rows[0:NVEC, :], ident[0:NVEC, 0:NVEC])
                elif g < 9:
                    pe.wait_ge(ld_x, 32)
                    for j, (t0, n) in enumerate(TOK_TILES):
                        ins = pe.transpose(bank[:, t0:t0 + n], rows[0:n, j, (g - 1) * P:g * P],
                                           ident[0:n, 0:n])
                elif g == 9:
                    pe.wait_ge(silu_c, 2)
                    for k in range(KT):
                        ins = pe.transpose(bank[:, k * SEQS:(k + 1) * SEQS], c_rows[:, k * P:(k + 1) * P],
                                           ident[0:SEQS, 0:SEQS])
                elif g == 10:
                    pe.wait_ge(ld_taps, 16)
                    for c in range(CT_):
                        ins = pe.transpose(bank[:, c * TAPS:(c + 1) * TAPS], tap_rows[:, c * P:(c + 1) * P],
                                           ident[0:TAPS, 0:TAPS])
                elif g < 15:
                    pe.wait_ge(ld_state, 32)
                    for j in range(2):
                        ins = pe.transpose(bank[:, j * 120:(j + 1) * 120],
                                           sconv_rows[:, j, (g - 11) * P:(g - 10) * P], ident[0:120, 0:120])
                else:
                    for c in range(CT_):
                        ins = pe.transpose(bank[:, c * 120:(c + 1) * 120], spool_rows[:, c * P:(c + 1) * P],
                                           ident[0:120, 0:120])
                ins.then_inc(turned, 1)

            def channel_sums(bank, src, weight, tiles, ready, done):
                for k in range(tiles):
                    if ready is not None:
                        pe.wait_ge(ready, k + 1)
                    ins = pe.matmul(ps[:, bank, 0:NT], avg[:, weight, :], src[:, k, :],
                                    start=(k == 0), stop=(k == tiles - 1))
                ins.then_inc(done, 1)

            def modulation(i, bank, first):
                c = MIX_AT["ada", i]
                w = chunk(c, KT)
                chunk_landed(c)
                for m in range(4):
                    at = (4 * i + m - first) * SEQS
                    for k in range(KT):
                        ins = pe.matmul(ps[:, bank, at:at + SEQS], w[:, k, m * P:(m + 1) * P],
                                        silc[:, k, :], start=(k == 0), stop=(k == KT - 1))
                ins.then_inc(chunk_used, 1)

            pe.wait_ge(turn_out, 11)
            channel_sums(1, sq, 0, KT, sq1, stat1)
            for i in range(4):
                modulation(i, 2, 0)

            pe.wait_ge(h1, KT)
            for i in range(7):
                c = MIX_AT["in", i]
                w = chunk(c, KT)
                chunk_landed(c)
                for m in range(4):
                    t = 4 * i + m
                    if t >= 8:
                        pe.wait_ge(z_out, t - 7)
                    for k in range(KT):
                        ins = pe.matmul(ps[:, t % 8, 0:NT], w[:, k, m * P:(m + 1) * P], hT[:, k, :],
                                        start=(k == 0), stop=(k == KT - 1))
                    ins.then_inc(z_done, 1)
                pe.wait_ge(z_done, 4 * i + 4)
                pe.sem_inc(chunk_used, 1)

            pe.wait_ge(u_ready, CT_)
            for i, (src, t0, t1) in enumerate(((uT, SEQ - CBUF, SEQ), (uT, SEQ, NT),
                                               (upT, SEQ - PBUF, SEQ), (upT, SEQ, NT))):
                pe.wait_ge(z_out, 25 + i)
                for c in range(CT_):
                    ins = pe.transpose(ps[0:t1 - t0, i, c * P:(c + 1) * P], src[:, c, t0:t1], ident[:, :])
                ins.then_inc(st_turned, 1)

            pe.wait_ge(v_ready, 2 * CT_ * TAPS)
            channel_sums(4, vT, 1, CT_, None, mean_done)
            modulation(4, 6, 16)
            pe.wait_ge(vsq, 1)
            channel_sums(5, gateT, 1, CT_, None, var_done)
            modulation(5, 6, 16)

            pe.wait_ge(ld_late, 48)
            pe.wait_ge(pooled, 4 * CT_)
            for t in range(KT):
                if t < 4:
                    pe.wait_ge(st_out, t + 1)
                else:
                    pe.wait_ge(yp_out, t - 3)
                pe.matmul(ps[:, t % 4, 0:NT], wpool[:, t // 2, (t % 2) * P:(t % 2 + 1) * P], upT[:, t // 2, :],
                          start=True, stop=True).then_inc(yp_done, 1)

            c = MIX_AT["conv_out", 0]
            w = chunk(c, CT_)
            chunk_landed(c)
            pe.wait_ge(vact, CT_)
            for t in range(KT):
                if t < 4:
                    pe.wait_ge(yp_out, t + 5)
                else:
                    pe.wait_ge(m_ready, t - 3)
                for k in range(CT_):
                    ins = pe.matmul(ps[:, t % 4, 0:NT], w[:, k, t * P:(t + 1) * P], vT[:, k, :],
                                    start=(k == 0), stop=(k == CT_ - 1))
                ins.then_inc(yc_done, 1)
            pe.wait_ge(yc_done, KT)
            pe.sem_inc(chunk_used, 1)
            modulation(6, 7, 24)
            modulation(7, 7, 24)

            pe.wait_ge(m_ready, KT)
            for i in range(2):
                c = MIX_AT["out", i]
                w = chunk(c, KT)
                chunk_landed(c)
                for m in range(4):
                    t = 4 * i + m
                    if t >= 4:
                        pe.wait_ge(x2_out, t - 3)
                    for k in range(KT):
                        ins = pe.matmul(ps[:, t % 4, 0:NT], w[:, k, m * P:(m + 1) * P], hT[:, k, :],
                                        start=(k == 0), stop=(k == KT - 1))
                    ins.then_inc(yo_done, 1)
                pe.wait_ge(yo_done, 4 * i + 4)
                pe.sem_inc(chunk_used, 1)
            modulation(8, 7, 24)
            modulation(9, 7, 24)
            channel_sums(4, sq, 0, KT, sq2, stat2)
            modulation(10, 6, 40)
            modulation(11, 6, 40)

            pe.wait_ge(h2, KT)
            for j, (t0, n) in enumerate(TOK_TILES):
                for k in range(KT):
                    ins = pe.matmul(ps[0:n, 5, j * NE:(j + 1) * NE], hT[:, k, t0:t0 + n], wrouter[:, k, :],
                                    start=(k == 0), stop=(k == KT - 1))
            ins.then_inc(logits, 1)
            for j, (t0, n) in enumerate(TOK_TILES):
                for half in range(2):
                    i = 2 * j + half
                    for q in range(4):
                        k = 4 * half + q
                        ins = pe.transpose(ps[0:n, (0, 1, 2, 3, 4, 7)[i], q * P:(q + 1) * P],
                                           hT[:, k, t0:t0 + n], ident[:, :])
                    ins.then_inc(h2_turned, 1)
            pe.wait_ge(mask_ready, 1)
            for j in range(NJ):
                for i in range(j + 1):
                    pe.matmul(ps[:, 6, j * NE:(j + 1) * NE], upper[:, :] if i == j else ones[:, :],
                              mask[:, i, :], start=(i == 0), stop=(i == j))
            for i in range(NJ):
                ins = pe.matmul(ps[:, 6, NJ * NE:(NJ + 1) * NE], ones[:, :], mask[:, i, :],
                                start=(i == 0), stop=(i == NJ - 1))
            ins.then_inc(ranked, 1)
            pe.wait_ge(wgt_ready, 1)
            for j, (t0, n) in enumerate(TOK_TILES):
                ins = pe.transpose(ps[0:NE, 5, t0:t0 + n], wgt[0:n, j, :], ident[0:n, 0:n])
            ins.then_inc(wT_turned, 1)
            pe.wait_ge(wT_out, 1)
            pe.wait_ge(h2_out, 6)
            pe.wait_ge(ld_bdown, 16)
            for t in range(KT):
                if t >= 4:
                    pe.wait_ge(bd_out, t - 3)
                pe.matmul(ps[:, BD_BANKS[t % 4], 0:NT], bdown[:, t * P:(t + 1) * P], wT[:, :],
                          start=True, stop=True).then_inc(bd_done, 1)

            def by_width(count, emit):
                with pe.If(count > WIDTHS[1]):
                    emit(SLOTS)
                with pe.Else():
                    with pe.If(count > WIDTHS[0]):
                        emit(WIDTHS[1])
                    with pe.Else():
                        emit(WIDTHS[0])

            def gather():
                for k in range(KT):
                    for j, (_, n) in enumerate(TOK_TILES):
                        at = (k % 4) * SLOTS
                        ins = pe.matmul(ps[:, HG_BANK + k // 4, at:at + SLOTS], rows[0:n, j, k * P:(k + 1) * P],
                                        hot[0:n, j, :], start=(j == 0), stop=(j == NJ - 1))
                ins.then_inc(gathered, 1)

            def tile_of(m, width):
                blocks = 4 * width // SLOTS
                return m // blocks, m % blocks

            def products(j, width, tokens, bias_at=None):
                w = chunk(NMIX + j, KT)
                tiles = SLOTS // width
                cols = COLS // tiles
                for k in range(KT):
                    for a in range(tiles):
                        ins = pe.matmul(ps[a * width:(a + 1) * width, UP_BANKS[j], 0:cols], tokens(k),
                                        w[:, k, a * cols:(a + 1) * cols],
                                        start=(k == 0), stop=(k == KT - 1 and bias_at is None))
                if bias_at is not None:
                    for a in range(tiles):
                        at = bias_at + a * cols
                        ins = pe.matmul(ps[a * width:(a + 1) * width, UP_BANKS[j], 0:cols],
                                        sel[:, 0:width], bup[:, at:at + cols], start=False, stop=True)
                ins.then_inc(chunk_used, 1)

            def expert_chunk_landed(n, j):
                c = NMIX + j
                pe.wait_ge(landed[c % RING], n * 16 + 16 * (c // RING + 1))

            def up(n, width):
                for j, at in enumerate((0, D, COLS, D + COLS)):
                    expert_chunk_landed(n, j)
                    if j == 3:
                        pe.wait_ge(glu_out, 2 * n + 1)
                    products(j, width, lambda k: hgT[:, k, 0:width], at)

            def turn_o(n, r, width):
                pe.wait_ge(added, KT * r + 9)
                for h in range(2):
                    pe.wait_ge(o_ready, 2 * n + h + 1)
                    for b in range(4 * width // SLOTS):
                        ins = pe.transpose(ps[:, T_BANK + h, b * P:(b + 1) * P],
                                           otok[:, h, b * P:(b + 1) * P], ident[:, :])
                    ins.then_inc(o_turned, 1)

            def down(n, width):
                def tokens(k):
                    a, b = tile_of(k % 4, width)
                    return oT[:, k // 4, b * P + a * width:b * P + (a + 1) * width]

                pe.wait_ge(oT_out, 2 * n + 2)
                for j in (4, 5):
                    expert_chunk_landed(n, j)
                    products(j, width, tokens)

            def combine(r, c, width):
                pe.wait_ge(comb_out, c)
                for i, k in enumerate(SUM_ORDER):
                    if i >= 3:
                        pe.wait_ge(added, KT * r + i - 1)
                    a, b = tile_of(k % 4, width)
                    at = (k // 4) * BANK + b * P
                    part = slice(a * width, (a + 1) * width)
                    pe.matmul(ps[:, T_BANK + i % 3, 0:NT], yrow[part, at:at + P], comb[part, :],
                              start=True, stop=True).then_inc(combined, 1)

            def expert_pass(n0, p, fixed):
                def sized(count, emit):
                    if fixed:
                        emit(SLOTS)
                    else:
                        by_width(count, emit)

                pe.wait_ge(hot_ready, p * GAT + 1)
                gather()
                with pe.Fori(0, NE) as e:
                    n = n0 + e
                    last = this = None
                    if not fixed:
                        last = pe.value_load(cnti[0:1, bass.ds(e, 1)], min_val=0, max_val=NT)
                        this = pe.value_load(cnti[0:1, bass.ds(e + 1, 1)], min_val=0, max_val=NT)
                    pe.wait_ge(hg_out, p * GAT + e + 1)
                    pe.wait_ge(sel_ready, p * GAT + e + 1)
                    pe.wait_ge(y_out, 2 * n + 1)
                    sized(this, lambda width: up(n, width))
                    pe.wait_ge(hot_ready, p * GAT + e + 2)
                    gather()
                    sized(last, lambda width: combine(p * GAT + e, p * GAT + e + 1, width))
                    pe.wait_ge(hotw_ready, n + 1)
                    pe.wait_ge(added, KT * (p * GAT + e) + 7)
                    for j, (t0, nt) in enumerate(TOK_TILES):
                        ins = pe.transpose(ps[:, T_BANK + 2, t0:t0 + nt], hotw[0:nt, j, :], ident[0:nt, 0:nt])
                    ins.then_inc(comb_turned, 1)
                    sized(this, lambda width: (turn_o(n, p * GAT + e, width), down(n, width)))
                pe.wait_ge(y_out, 2 * n0 + 2 * NE + 1)
                last = None if fixed else pe.value_load(cnti[0:1, NE:NE + 1], min_val=0, max_val=NT)
                sized(last, lambda width: combine(p * GAT + NE, p * GAT + NE + 1, width))

            pe.wait_ge(ld_bup, 16)
            pe.wait_ge(turn_clear, 1)
            pe.wait_ge(added, 1)
            expert_pass(0, 0, False)
            most = pe.value_load(cnti[0:1, NE + 2:NE + 3], min_val=0, max_val=NT)
            with pe.If(most > SLOTS):
                with pe.Fori(1, PASSES) as p:
                    expert_pass(p * NE, p, True)

            channel_sums(0, sq, 0, KT, sq3, stat3)
            pe.wait_ge(yn, KT)
            for j, (t0, n) in enumerate(TOK_TILES):
                for half in range(2):
                    for q in range(4):
                        ins = pe.transpose(ps[0:n, 1 + 2 * j + half, q * P:(q + 1) * P],
                                           hT[:, 4 * half + q, t0:t0 + n], ident[:, :])
                    ins.then_inc(fin_turned, 1)


_INS = ['x_prompt', 'x_sample', 'state_conv', 'state_pool', 'c_prompt', 'c_sample', 'w_ada', 'b_ada',
        'norm_mix', 'w_in', 'b_in', 'conv_w', 'conv_b', 'conv_ln_g', 'conv_ln_b', 'w_conv_out', 'w_pool',
        'pool_scale', 'w_out', 'norm_ffn', 'w_router', 'b_router', 'w_up', 'b_up', 'w_down', 'b_down',
        'norm_final']
_OUTS = [(1, SEQ, D), (DEC_B, DEC_T, D), (1, 1, CBUF, DC), (1, 1, PBUF, DC),
         (1, DEC_B, CBUF, DC), (1, DEC_B, PBUF, DC)]


def kernel(**inputs):
    import numpy as np
    import concourse.bacc as bacc
    from concourse.bass_utils import run_bass_kernel_spmd

    nc = bacc.Bacc("TRN2", target_bir_lowering=False, num_devices=1)
    arrays, args = {}, []
    for name in _INS:
        a = np.ascontiguousarray(inputs[name])
        arrays[f"in_{name}_dram"] = a
        args.append(nc.dram_tensor(f"in_{name}_dram", a.shape, mybir.dt.from_np(a.dtype),
                                   kind="ExternalInput").ap())
    for i, shape in enumerate(_OUTS):
        args.append(nc.dram_tensor(f"out_{i}_dram", shape, F32, kind="ExternalOutput").ap())
    build(nc, *args)
    r = run_bass_kernel_spmd(nc, [arrays], core_ids=[0])
    return tuple(r.results[0][f"out_{i}_dram"] for i in range(len(_OUTS)))
```

```python
from contextlib import ExitStack

import concourse.bass as bass
from concourse import mybir

P = 128
F32 = mybir.dt.float32
I32 = mybir.dt.int32
ALU = mybir.AluOpType
ACT = mybir.ActivationFunctionType
AX = mybir.AxisListType

D = 1024
KT = D // P
SEQ = 256
DEC_B, DEC_T = 8, 4
DEC = DEC_B * DEC_T
NT = SEQ + DEC
SEQS = 1 + DEC_B
TOK_TILES = [(0, P), (P, P), (2 * P, NT - 2 * P)]
NJ = len(TOK_TILES)
DC = D // 2
CT_ = DC // P
TAPS = 31
CBUF = TAPS - 1
WINDOWS = (2, 4, 8, 16)
PBUF = max(WINDOWS) - 1
NE = 32
TOPK = 4
LIMIT = 7.0
ALPHA = 1.702
EPS = 1e-6

SLOTS = 128
CW = 32
MOD_CHUNKS = 4
NARROW = 64
NH = SLOTS // NARROW
PASSES = (NT + SLOTS - 1) // SLOTS

RING = 6
COLS = 512
BANK = 512

MIXER_CHUNKS = ([("ada", i) for i in range(4)] + [("in", i) for i in range(7)] +
                [("ada", i) for i in range(4, 8)] + [("conv_out", 0), ("out", 0), ("out", 1)] +
                [("ada", i) for i in range(8, 12)])
NMIX = len(MIXER_CHUNKS)
MIX_AT = {c: i for i, c in enumerate(MIXER_CHUNKS)}
EXPERT_CHUNKS = 6
EXPERT_RING = (6, 7) + tuple((NMIX - RING + i) % RING for i in range(RING))
NRING = len(EXPERT_RING)
UNROLL = 4
TURNS = UNROLL * EXPERT_CHUNKS // NRING
assert TURNS * NRING == UNROLL * EXPERT_CHUNKS and NE % UNROLL == 0
MIXER_USES = [len(range(s, NMIX, RING)) if s < RING else 0 for s in range(NRING)]

VEC_ROWS = {}
_at = 0
for _name, _n in (("b_ada", 48), ("b_in", 28), ("norm_mix", 8), ("norm_ffn", 8), ("norm_final", 8),
                  ("pool_scale", 8), ("conv_b", 4), ("conv_ln_g", 4), ("conv_ln_b", 4)):
    VEC_ROWS[_name] = (_at, _n)
    _at += _n
NVEC = _at

PF_W = (PBUF + SEQ) + DEC_B * (PBUF + DEC_T)
UF_W = (CBUF + SEQ) + DEC_B * (CBUF + DEC_T)


def build(nc, x_prompt, x_sample, state_conv, state_pool, c_prompt, c_sample, w_ada, b_ada, norm_mix,
          w_in, b_in, conv_w, conv_b, conv_ln_g, conv_ln_b, w_conv_out, w_pool, pool_scale, w_out,
          norm_ffn, w_router, b_router, w_up, b_up, w_down, b_down, norm_final,
          y_prompt, y_sample, new_conv_prompt, new_pool_prompt, new_conv_sample, new_pool_sample):
    with ExitStack() as ctx:
        def sb(name, shape, dt=F32):
            return ctx.enter_context(nc.sbuf_tensor(name, shape, dt))

        def sem(name):
            return ctx.enter_context(nc.semaphore(name))

        ring = sb("ring", [P, RING, KT * COLS])
        vec = sb("vec", [P, P])
        taps = sb("taps", [P, CT_, TAPS])
        rows = sb("rows", [P, NJ, D])
        wrouter = sb("wrouter", [P, KT, NE])
        wpool = sb("wpool", [P, CT_, 2 * P])
        xT = sb("xT", [P, KT, NT])
        hT = sb("hT", [P, KT, NT])
        sq = sb("sq", [P, KT, NT])
        uv = sb("uv", [P, KT, NT])
        sg = sb("sg", [P, 2 * KT * NT])
        ufull = sb("ufull", [P, CT_ * UF_W])
        pbuf = sb("pbuf", [P, 3 * CT_ * PF_W])
        modT = sb("modT", [P, 6 * KT, SEQS])
        silc = sb("silc", [P, KT, CW])
        rtab = sb("rtab", [P, NH, NJ, NE + 1])
        sel = sb("sel", [P, SLOTS])
        ident = sb("ident", [P, P])
        upper = sb("upper", [P, P])
        ones = sb("ones", [P, P])
        avg = sb("avg", [P, 2, P])
        epsc = sb("epsc", [P, 1])
        rms = sb("rms", [P, NT])
        rstd = sb("rstd", [P, NT])
        iota = sb("iota", [P, SLOTS])
        icnt = sb("icnt", [P, CT_, 16])
        brout = sb("brout", [P, NE])
        top8 = sb("top8", [P, NJ, 8])
        need = sb("need", [P, NJ])
        wgt = sb("wgt", [P, NJ, NE])
        rankm = sb("rankm", [P, NJ, NE + 1])
        cntf = sb("cntf", [1, NE + 3])
        cnti = sb("cnti", [1, NE + 3], I32)

        pf, pa, pb = (pbuf[:, i * CT_ * PF_W:(i + 1) * CT_ * PF_W] for i in range(3))
        sqf = sq[:, :, :].rearrange("p k n -> p (k n)")
        tap_rows = pa[0:TAPS, 0:DC]
        vec_rows = pb[:, 0:P]
        bdown = wpool[0:NE, :, :].rearrange("p g n -> p (g n)")
        wT = sqf[0:NE, 0:NT]
        lg, mask, eq, cum = (ufull[:, a:a + NJ * NE].rearrange("p (j e) -> p j e", e=NE)
                             for a in range(2 * NJ * SLOTS + NT, 2 * NJ * SLOTS + NT + 4 * NJ * NE, NJ * NE))

        a = 2 * NJ * SLOTS + NT + 4 * NJ * NE
        starts = ufull[:, a:a + NH * NE].rearrange("p (q e) -> p q e", e=NE)

        sconv_rows = sg[0:120, 2 * D:2 * D + 2 * DC].rearrange("p (j d) -> p j d", j=2)
        c_rows = sg[0:SEQS, 3 * D:4 * D]
        spool_rows = sg[0:120, 4 * D:4 * D + DC]
        sgT = sg[:, :].rearrange("p (t n) -> p t n", n=NT)
        SLOT = KT * COLS
        slots = [ring[:, s, :] for s in range(RING)] + [pbuf[:, 0:SLOT], sg[:, 0:SLOT]]
        hgT = sqf[:, 0:KT * SLOTS].rearrange("p (h n) -> p h n", h=2)
        yrow = sqf[:, KT * SLOTS:2 * KT * SLOTS]
        hot = ufull[:, 0:NJ * SLOTS].rearrange("p (j s) -> p j s", s=SLOTS)
        hotw = ufull[:, NJ * SLOTS:2 * NJ * SLOTS].rearrange("p (j s) -> p j s", s=SLOTS)
        comb = ufull[:, 2 * NJ * SLOTS:2 * NJ * SLOTS + NT]
        a = 2 * NJ * SLOTS + NT
        oT = ufull[:, a:a + KT * SLOTS].rearrange("p (h n) -> p h n", h=2)
        bup = hT[:, :, :].rearrange("p k n -> p (k n)")[:, 0:2 * D]
        glu = sg[:, SLOT:SLOT + BANK]
        sig = pbuf[:, SLOT:SLOT + BANK]
        otok = wpool[:, :, :].rearrange("p g n -> p (g n)").rearrange("p (h n) -> p h n", h=2)
        uf = ufull[:, :].rearrange("p (c n) -> p c n", c=CT_)
        uf_p = uf[:, :, 0:CBUF + SEQ]
        uf_s = uf[:, :, CBUF + SEQ:UF_W].rearrange("p c (s t) -> p c s t", s=DEC_B)
        pool_bufs = []
        for buf in (pf, pa, pb):
            v = buf[:, :].rearrange("p (c n) -> p c n", c=CT_)
            pool_bufs.append((v[:, :, 0:PBUF + SEQ],
                              v[:, :, PBUF + SEQ:PF_W].rearrange("p c (s t) -> p c s t", s=DEC_B)))
        mod_rows_of = (sg[:, 0:BANK], pbuf[:, SLOT:SLOT + BANK], pbuf[:, SLOT:SLOT + BANK])
        uT = uv[:, 0:CT_, :]
        vT = uv[:, CT_:KT, :]
        accT = uv
        gateT = sq[:, 0:CT_, :]
        upT = sq[:, CT_:KT, :]
        stage = rows[:, :, :].rearrange("p j d -> p (j d)")

        def vcol(name, i):
            return vec[:, VEC_ROWS[name][0] + i:VEC_ROWS[name][0] + i + 1]

        def vcols(name):
            a, n = VEC_ROWS[name]
            return vec[:, a:a + n]

        def decoded(ap):
            return ap[:, :, SEQ:NT].rearrange("p k (s t) -> p k s t", t=DEC_T)

        ps = ctx.enter_context(nc.psum_tensor("ps", [P, 8, BANK], F32))

        ld_vec = sem("ld_vec")
        ld_x = sem("ld_x")
        ld_c = sem("ld_c")
        ld_taps = sem("ld_taps")
        ld_state = sem("ld_state")
        ld_bup = sem("ld_bup")
        bup_clear = sem("bup_clear")
        sel_ready = sem("sel_ready")
        ld_late = sem("ld_late")
        ld_bdown = sem("ld_bdown")
        landed = [sem(f"landed{i}") for i in range(NRING)]
        chunk_used = sem("chunk_used")
        consts = sem("consts")
        zeroed = sem("zeroed")
        silu_c = sem("silu_c")
        turned = sem("turned")
        mod_rows = sem("mod_rows")
        mod_turned = sem("mod_turned")
        turn_out = sem("turn_out")
        sq1 = sem("sq1")
        stat1 = sem("stat1")
        rms1 = sem("rms1")
        h1 = sem("h1")
        z_done = sem("z_done")
        z_out = sem("z_out")
        u_ready = sem("u_ready")
        uf_ready = sem("uf_ready")
        v_ready = sem("v_ready")
        st_turned = sem("st_turned")
        st_out = sem("st_out")
        pool_step = sem("pool_step")
        pooled = sem("pooled")
        mean_done = sem("mean_done")
        centred = sem("centred")
        vsq = sem("vsq")
        var_done = sem("var_done")
        vrms = sem("vrms")
        ln_ready = sem("ln_ready")
        ln_sig = sem("ln_sig")
        vact = sem("vact")
        yp_done = sem("yp_done")
        yp_out = sem("yp_out")
        yc_done = sem("yc_done")
        m_ready = sem("m_ready")
        yo_done = sem("yo_done")
        x2_out = sem("x2_out")
        sq2 = sem("sq2")
        stat2 = sem("stat2")
        rms2 = sem("rms2")
        h2 = sem("h2")
        logits = sem("logits")
        h2_turned = sem("h2_turned")
        h2_out = sem("h2_out")
        shifted = sem("shifted")
        expd = sem("expd")
        mask_ready = sem("mask_ready")
        wgt_ready = sem("wgt_ready")
        ranked = sem("ranked")
        rank_ready = sem("rank_ready")
        wT_turned = sem("wT_turned")
        wT_out = sem("wT_out")
        bd_done = sem("bd_done")
        bd_out = sem("bd_out")
        turn_clear = sem("turn_clear")
        pass_ready = sem("pass_ready")
        hot_ready = sem("hot_ready")
        hotw_ready = sem("hotw_ready")
        gathered = sem("gathered")
        grow_out = sem("grow_out")
        g_turned = sem("g_turned")
        hg_out = sem("hg_out")
        glu_out = sem("glu_out")
        sig_out = sem("sig_out")
        lin_clip = sem("lin_clip")
        gs_out = sem("gs_out")
        o_ready = sem("o_ready")
        y_out = sem("y_out")
        o_turned = sem("o_turned")
        oT_out = sem("oT_out")
        combined = sem("combined")
        added = sem("added")
        comb_turned = sem("comb_turned")
        comb_out = sem("comb_out")
        x3_out = sem("x3_out")
        sq3 = sem("sq3")
        stat3 = sem("stat3")
        rms3 = sem("rms3")
        yn = sem("yn")
        fin_turned = sem("fin_turned")
        fin_out = sem("fin_out")
        st_sent = sem("st_sent")
        old_sent = sem("old_sent")
        y_sent = sem("y_sent")
        dve_done = sem("dve_done")
        pool_done = sem("pool_done")

        UP_BANKS = (0, 1, 2, 0, 1, 2)
        HG_BANK = 3
        T_BANK = 5
        BD_BANKS = (0, 1, 2, 7)
        SUM_ORDER = (0, 2, 1, 3, 4, 6, 5, 7)
        GAT = NE + 1

        block = ctx.enter_context(nc.Block())

        @block.sync
        def _(sp):
            def late_loads():
                sp.dma_start(tap_rows[:, :], conv_w[0]).then_inc(ld_taps, 16)
                sp.dma_start(sconv_rows, state_conv[0].rearrange("s t d -> (s t) d")
                              .rearrange("(j p) d -> p j d", j=2)).then_inc(ld_state, 16)
                sp.dma_start(spool_rows, state_pool[0].rearrange("s t d -> (s t) d")).then_inc(ld_state, 16)
                sp.dma_start(wpool[:, :, :], w_pool[0].rearrange("g p n -> p g n")).then_inc(ld_late, 16)
                sp.dma_start(wrouter[:, :, :], w_router[0].rearrange("(k p) n -> p k n", p=P)).then_inc(ld_late, 16)
                sp.dma_start(brout[:, :], b_router.broadcast_to([P, NE])).then_inc(ld_late, 16)

            def source(kind, i):
                cols = slice(i * COLS, (i + 1) * COLS)
                if kind == "conv_out":
                    return w_conv_out[0].rearrange("(k p) n -> p k n", p=P)
                w = {"ada": w_ada, "in": w_in, "out": w_out}[kind]
                return w[0].rearrange("(k p) n -> p k n", p=P)[:, :, cols]

            sp.dma_start(rows[:, 0:2, :], x_prompt[0].rearrange("(j p) d -> p j d", p=P)).then_inc(ld_x, 16)
            sp.dma_start(rows[0:DEC, 2, :], x_sample.rearrange("b t d -> (b t) d")).then_inc(ld_x, 16)
            sp.dma_start(c_rows[0:1, :], c_prompt).then_inc(ld_c, 16)
            sp.dma_start(c_rows[1:SEQS, :], c_sample).then_inc(ld_c, 16)
            for name, ap in (("b_ada", b_ada[0]), ("b_in", b_in[0]), ("norm_mix", norm_mix[0]),
                             ("norm_ffn", norm_ffn[0]), ("norm_final", norm_final),
                             ("pool_scale", pool_scale[0]), ("conv_b", conv_b[0]),
                             ("conv_ln_g", conv_ln_g[0]), ("conv_ln_b", conv_ln_b[0])):
                a, n = VEC_ROWS[name]
                sp.dma_start(vec_rows[a:a + n, :], ap.rearrange("(r p) -> r p", p=P)).then_inc(ld_vec, 16)
            for c, (kind, i) in enumerate(MIXER_CHUNKS):
                if c == 1:
                    late_loads()
                if c >= RING:
                    sp.wait_ge(chunk_used, c - RING + 1)
                src = source(kind, i)
                dst = ring[:, c % RING, :].rearrange("p (k n) -> p k n", k=src.shape[1])
                sp.dma_start(dst, src).then_inc(landed[c % RING], 16)

            up = w_up[0].rearrange("e (k p) n -> e p k n", p=P)
            down = w_down[0].rearrange("e (k p) n -> e p k n", p=P)
            parts = ((up, 0), (up, D), (up, COLS), (up, D + COLS), (down, 0), (down, COLS))

            def expert_weights(n0, step):
                for u in range(UNROLL):
                    e = step * UNROLL + u
                    for j, (w, col) in enumerate(parts):
                        i = u * EXPERT_CHUNKS + j
                        slot = EXPERT_RING[i % NRING]
                        sp.wait_ge(chunk_used, (n0 + step * UNROLL) * EXPERT_CHUNKS + (NMIX + i - NRING + 1))
                        sp.dma_start(slots[slot].rearrange("p (k n) -> p k n", k=KT),
                                     w[e, :, :, col:col + COLS]).then_inc(landed[slot], 16)

            sp.wait_ge(pooled, 4 * CT_)
            sp.wait_ge(m_ready, KT)
            with sp.Fori(0, NE // UNROLL) as step:
                expert_weights(0, step)
            sp.wait_ge(rank_ready, 1)
            most = sp.value_load(cnti[0:1, NE + 2:NE + 3], min_val=0, max_val=NT)
            with sp.If(most > SLOTS):
                with sp.Fori(1, PASSES) as p:
                    with sp.Fori(0, NE // UNROLL) as step:
                        expert_weights(p * NE, step)

            sp.wait_ge(fin_out, 2)
            sp.dma_start(y_prompt[0, 0:P, :], rows[:, 0, :]).then_inc(y_sent, 16)
            sp.wait_ge(fin_out, 4)
            sp.dma_start(y_prompt[0, P:2 * P, :], rows[:, 1, :]).then_inc(y_sent, 16)
            sp.wait_ge(fin_out, 6)
            sp.dma_start(y_sample.rearrange("b t d -> (b t) d"), rows[0:DEC, 2, :]).then_inc(y_sent, 16)
            sp.wait_ge(y_sent, 3 * 16)
            sp.wait_ge(st_sent, 16 * (2 + 2 * DEC_B))

        @block.gpsimd
        def _(pool):
            pool.memset(ident[:, :], 0.0).then_inc(zeroed, 1)
            pool.memset(upper[:, :], 0.0).then_inc(zeroed, 1)
            pool.memset(ones[:, :], 1.0).then_inc(consts, 1)
            pool.memset(avg[:, 0, :], 1.0 / D).then_inc(consts, 1)
            pool.memset(avg[:, 1, :], 1.0 / DC).then_inc(consts, 1)
            pool.memset(epsc[:, :], EPS).then_inc(consts, 1)
            pool.wait_ge(zeroed, 2)
            pool.affine_select(out=ident[:, :], in_=ident[:, :], compare_op=ALU.not_equal, fill=1.0,
                               base=0, pattern=[[-1, P]], channel_multiplier=1).then_inc(consts, 1)
            pool.affine_select(out=upper[:, :], in_=upper[:, :], compare_op=ALU.is_ge, fill=1.0,
                               base=0, pattern=[[-1, P]], channel_multiplier=1).then_inc(consts, 1)
            pool.dma_start(new_conv_sample[0, :, 0:CBUF - DEC_T, :],
                           state_conv[0, :, DEC_T:CBUF, :]).then_inc(old_sent, 16)
            pool.dma_start(new_pool_sample[0, :, 0:PBUF - DEC_T, :],
                           state_pool[0, :, DEC_T:PBUF, :]).then_inc(old_sent, 16)
            pool.iota(iota[:, :], pattern=[[1, SLOTS]], base=0, channel_multiplier=0,
                      allow_small_or_imprecise_dtypes=True).then_inc(consts, 1)
            pool.iota(icnt[:, :, :], pattern=[[0, CT_], [1, 16]], base=1, channel_multiplier=0,
                      allow_small_or_imprecise_dtypes=True).then_inc(pool_done, 1)
            pool.wait_ge(pool_done, 1)
            for g, w in enumerate(WINDOWS):
                pool.tensor_scalar(icnt[:, g, :], icnt[:, g, :], float(w), None, ALU.min)\
                    .then_inc(consts, 1)
            (f_p, f_s), (a_p, a_s), (b_p, b_s) = pool_bufs
            pool.memset(f_p[:, :, 0:PBUF], 0.0).then_inc(pool_step, 1)
            pool.wait_ge(z_out, 3 * CT_)
            pool.wait_ge(turn_out, 16)
            pool.tensor_copy(f_p[:, :, PBUF:PBUF + SEQ], upT[:, :, 0:SEQ]).then_inc(pool_step, 1)
            for g in range(CT_):
                pool.tensor_copy(f_s[:, g, :, PBUF:PBUF + DEC_T],
                                 upT[:, g, SEQ:NT].rearrange("p (s t) -> p s t", t=DEC_T))\
                    .then_inc(pool_step, 1)
            pool.wait_ge(pool_step, 2 + CT_)
            src, dst = (f_p, f_s), (a_p, a_s)
            for g, w in enumerate(WINDOWS):
                lag, first = w // 2, w - 1
                pool.tensor_tensor(dst[0][:, g:, first:], src[0][:, g:, first:],
                                   src[0][:, g:, first - lag:PBUF + SEQ - lag], ALU.add)\
                    .then_inc(pool_step, 1)
                for q in range(g, CT_):
                    pool.tensor_tensor(dst[1][:, q, :, first:], src[1][:, q, :, first:],
                                       src[1][:, q, :, first - lag:PBUF + DEC_T - lag], ALU.add)\
                        .then_inc(pool_step, 1)
                pool.wait_ge(pool_step, 2 + CT_ + (g + 1) + sum(CT_ - q for q in range(g + 1)))
                src, dst = dst, ((b_p, b_s) if g % 2 == 0 else (a_p, a_s))

            pool.wait_ge(old_sent, 32)
            pool.wait_ge(yp_done, KT)
            pool.dma_start(bdown, b_down[0]).then_inc(ld_bdown, 16)
            pool.wait_ge(h2_turned, 2 * NJ)
            pool.memset(bup, 0.0).then_inc(bup_clear, 1)
            pool.wait_ge(bup_clear, 1)
            pool.dma_start(bup[0:NE, :], b_up[0]).then_inc(ld_bup, 16)

        @block.scalar
        def _(act):
            act.wait_ge(ld_c, 32)
            act.activation(sq[0:SEQS, 0:4, 0:256], c_rows.rearrange("p (k n) -> p k n", k=4),
                           ACT.Sigmoid).then_inc(silu_c, 1)

            for k in range(KT):
                act.wait_ge(turn_out, k + 2)
                if k == 0:
                    act.wait_ge(silu_c, 2)
                act.activation(sq[:, k, :], xT[:, k, :], ACT.Square).then_inc(sq1, 1)
            act.wait_ge(stat1, 1)
            act.wait_ge(consts, 4)
            act.activation(rms[:, :], ps[:, 1, 0:NT], ACT.Sqrt, bias=epsc[:, :]).then_inc(rms1, 1)

            def mod_rows_out(g, bank):
                act.wait_ge(chunk_used, MIX_AT["ada", MOD_CHUNKS * (g + 1) - 1] + 1)
                act.copy(mod_rows_of[g], ps[:, bank, :]).then_inc(mod_rows, 1)

            mod_rows_out(0, 2)

            for t in range(28):
                act.wait_ge(z_done, t + 1)
                src, bias = ps[:, t % 8, 0:NT], vcol("b_in", t)
                if t < CT_:
                    act.activation(uT[:, t, :], src, ACT.Identity, bias=bias).then_inc(z_out, 1)
                elif t < 2 * CT_:
                    act.activation(gateT[:, t - CT_, :], src, ACT.Sigmoid, bias=bias).then_inc(z_out, 1)
                elif t < 3 * CT_:
                    act.activation(upT[:, t - 2 * CT_, :], src, ACT.Identity, bias=bias).then_inc(z_out, 1)
                else:
                    act.activation(sgT[:, t - 3 * CT_, :], src, ACT.Sigmoid, bias=bias).then_inc(z_out, 1)

            for i in range(4):
                n = (CBUF, DEC, PBUF, DEC)[i]
                act.wait_ge(st_turned, i + 1)
                act.copy(stage[0:n, i * DC:(i + 1) * DC], ps[0:n, i, :]).then_inc(st_out, 1)
            act.wait_ge(st_out, 4)
            act.dma_start(new_conv_prompt[0, 0], stage[0:CBUF, 0:DC]).then_inc(st_sent, 16)
            act.dma_start(new_pool_prompt[0, 0], stage[0:PBUF, 2 * DC:3 * DC]).then_inc(st_sent, 16)
            for s in range(DEC_B):
                act.dma_start(new_conv_sample[0, s, CBUF - DEC_T:CBUF, :],
                              stage[s * DEC_T:(s + 1) * DEC_T, DC:2 * DC]).then_inc(st_sent, 16)
                act.dma_start(new_pool_sample[0, s, PBUF - DEC_T:PBUF, :],
                              stage[s * DEC_T:(s + 1) * DEC_T, 3 * DC:4 * DC]).then_inc(st_sent, 16)

            act.wait_ge(centred, 1)
            act.activation(gateT, vT, ACT.Square).then_inc(vsq, 1)
            mod_rows_out(1, 6)
            act.wait_ge(var_done, 1)
            act.activation(rms[:, :], ps[:, 5, 0:NT], ACT.Sqrt, bias=epsc[:, :]).then_inc(vrms, 1)
            for c in range(CT_):
                act.wait_ge(ln_ready, c + 1)
                act.activation(gateT[:, c, :], vT[:, c, :], ACT.Sigmoid).then_inc(ln_sig, 1)

            for k in range(KT):
                act.wait_ge(x2_out, k + 1)
                act.activation(sq[:, k, :], xT[:, k, :], ACT.Square).then_inc(sq2, 1)
            mod_rows_out(2, 6)
            act.wait_ge(stat2, 1)
            act.activation(rms[:, :], ps[:, 4, 0:NT], ACT.Sqrt, bias=epsc[:, :]).then_inc(rms2, 1)

            act.wait_ge(st_sent, 16 * (2 + 2 * DEC_B))
            for j, (_, n) in enumerate(TOK_TILES):
                for half in range(2):
                    i = 2 * j + half
                    act.wait_ge(h2_turned, i + 1)
                    act.copy(rows[0:n, j, half * BANK:(half + 1) * BANK],
                             ps[0:n, (0, 1, 2, 3, 4, 7)[i], :]).then_inc(h2_out, 1)
            act.wait_ge(shifted, 1)
            act.activation(wgt[:, :, :], lg[:, :, :], ACT.Exp).then_inc(expd, 1)
            for t in range(KT):
                act.wait_ge(bd_done, t + 1)
                act.copy(accT[:, t, :], ps[:, BD_BANKS[t % 4], 0:NT]).then_inc(bd_out, 1)

            def gather_out(g):
                act.wait_ge(gathered, g)
                for h in range(2):
                    act.copy(yrow[:, h * BANK:(h + 1) * BANK], ps[:, HG_BANK + h, :]).then_inc(grow_out, 1)

            def gather_turned(g):
                for h in range(2):
                    act.wait_ge(g_turned, 2 * (g - 1) + h + 1)
                    act.copy(hgT[:, h, :], ps[:, HG_BANK + h, :]).then_inc(hg_out, 1)

            def expert_pass(n0, p):
                gather_out(p * GAT + 1)
                gather_turned(p * GAT + 1)
                with act.Fori(0, NE) as e:
                    n = n0 + e
                    for h in range(2):
                        act.wait_ge(glu_out, 2 * n + h + 1)
                        act.activation(sig, glu, ACT.Sigmoid, scale=ALPHA).then_inc(sig_out, 1)
                    gather_out(p * GAT + e + 2)
                    for h in range(2):
                        act.wait_ge(o_turned, 2 * n + h + 1)
                        act.copy(oT[:, h, :], ps[:, T_BANK + h, :]).then_inc(oT_out, 1)
                    gather_turned(p * GAT + e + 2)
                    for h in range(2):
                        act.wait_ge(chunk_used, NMIX + n * EXPERT_CHUNKS + 5 + h)
                        act.copy(yrow[:, h * BANK:(h + 1) * BANK], ps[:, UP_BANKS[4 + h], :])\
                            .then_inc(y_out, 1)

            expert_pass(0, 0)
            most = act.value_load(cnti[0:1, NE + 2:NE + 3], min_val=0, max_val=NT)
            with act.If(most > SLOTS):
                with act.Fori(1, PASSES) as p:
                    expert_pass(p * NE, p)

            for k in range(KT):
                act.wait_ge(x3_out, k + 1)
                act.activation(sq[:, k, :], xT[:, k, :], ACT.Square).then_inc(sq3, 1)
            act.wait_ge(stat3, 1)
            act.activation(rms[:, :], ps[:, 0, 0:NT], ACT.Sqrt, bias=epsc[:, :]).then_inc(rms3, 1)
            for j, (_, n) in enumerate(TOK_TILES):
                for half in range(2):
                    i = 2 * j + half
                    act.wait_ge(fin_turned, i + 1)
                    act.copy(rows[0:n, j, half * BANK:(half + 1) * BANK], ps[0:n, 1 + i, :])\
                        .then_inc(fin_out, 1)

        @block.vector
        def _(dve):
            step = [0]

            def link(ins):
                step[0] += 1
                ins.then_inc(dve_done, 1)
                dve.wait_ge(dve_done, step[0])

            V = nc.vector
            V.memset(uf_p[:, :, 0:CBUF], 0.0).then_inc(dve_done, 1)
            V.memset(rankm[:, :, NE:NE + 1], -1.0).then_inc(dve_done, 1)
            V.memset(silc[:, :, :], 0.0).then_inc(dve_done, 1)
            V.memset(cntf[:, :], 0.0).then_inc(dve_done, 1)
            step[0] = 4

            for g in range(16):
                dve.wait_ge(turned, g + 1)
                bank = ps[:, g % 8, :]
                if g == 0:
                    ins = V.tensor_copy(vec[:, 0:NVEC], bank[:, 0:NVEC])
                elif g < 9:
                    ins = V.tensor_copy(xT[:, g - 1, :], bank[:, 0:NT])
                elif g == 9:
                    dve.wait_ge(dve_done, 4)
                    ins = V.tensor_copy(silc[:, :, 0:SEQS], bank[:, 0:KT * SEQS].rearrange("p (k s) -> p k s", k=KT))
                elif g == 10:
                    ins = V.tensor_copy(taps[:, :, :], bank[:, 0:CT_ * TAPS].rearrange("p (c w) -> p c w", c=CT_))
                elif g < 15:
                    ins = V.tensor_copy(uf_s[:, g - 11, :, 0:CBUF],
                                        bank[:, 0:DEC_B * CBUF].rearrange("p (s t) -> p s t", t=CBUF))
                else:
                    for c in range(CT_):
                        ins = V.tensor_copy(pool_bufs[0][1][:, c, :, 0:PBUF],
                                            bank[:, c * 120:(c + 1) * 120].rearrange("p (s t) -> p s t", t=PBUF))
                ins.then_inc(turn_out, 1)
                if g == 0:
                    dve.wait_ge(silu_c, 1)
                    V.tensor_tensor(c_rows.rearrange("p (k n) -> p k n", k=4),
                                    c_rows.rearrange("p (k n) -> p k n", k=4),
                                    sq[0:SEQS, 0:4, 0:256], ALU.mult).then_inc(silu_c, 1)

            dve.wait_ge(consts, 11)
            link(V.reciprocal(icnt[:, :, :], icnt[:, :, :]))

            def mod_out(g, bank):
                a = VEC_ROWS["b_ada"][0]
                n = 2 * KT
                dve.wait_ge(mod_turned, g + 1)
                link(V.tensor_tensor(modT[:, g * n:(g + 1) * n, :],
                                     ps[:, bank, :].rearrange("p (t s) -> p t s", s=CW)[:, :, 0:SEQS],
                                     vec[:, a + g * n:a + (g + 1) * n].unsqueeze(2).to_broadcast([P, n, SEQS]),
                                     ALU.add))

            def gain(sc, norm):
                part = modT[:, sc * KT:(sc + 1) * KT, :]
                link(V.tensor_scalar(part, part, 1.0, None, ALU.add))
                link(V.tensor_tensor(part, part, vcols(norm).unsqueeze(2).to_broadcast([P, KT, SEQS]), ALU.mult))

            def per_seq(i):
                return modT[:, i * KT:(i + 1) * KT, 1:SEQS].unsqueeze(3).to_broadcast([P, KT, DEC_B, DEC_T])

            def modulate(sh, sc, ready):
                link(V.reciprocal(rstd[:, :], rms[:, :]))
                link(V.tensor_tensor(hT[:, :, :], xT[:, :, :],
                                     rstd[:, :].unsqueeze(1).to_broadcast([P, KT, NT]), ALU.mult))
                link(V.tensor_tensor(decoded(hT), decoded(hT), per_seq(sc), ALU.mult))
                link(V.tensor_tensor(decoded(hT), decoded(hT), per_seq(sh), ALU.add))
                for k in range(KT):
                    V.tensor_scalar(hT[:, k, 0:SEQ], hT[:, k, 0:SEQ], modT[:, sc * KT + k, 0:1],
                                    modT[:, sh * KT + k, 0:1], ALU.mult, ALU.add).then_inc(ready, 1)

            dve.wait_ge(turn_out, 16)
            mod_out(0, 3)
            gain(1, "norm_mix")
            dve.wait_ge(rms1, 1)
            modulate(0, 1, h1)

            for c in range(CT_):
                dve.wait_ge(z_out, CT_ + c + 1)
                V.tensor_tensor(uT[:, c, :], uT[:, c, :], gateT[:, c, :], ALU.mult).then_inc(u_ready, 1)
            for c in range(CT_):
                dve.wait_ge(u_ready, c + 1)
                V.tensor_copy(uf_p[:, c, CBUF:CBUF + SEQ], uT[:, c, 0:SEQ]).then_inc(uf_ready, 1)
                V.tensor_copy(uf_s[:, c, :, CBUF:CBUF + DEC_T],
                              uT[:, c, SEQ:NT].rearrange("p (s t) -> p s t", t=DEC_T)).then_inc(uf_ready, 1)
            dve.wait_ge(uf_ready, 2 * CT_)
            for w in range(TAPS):
                for c in range(CT_):
                    for q, (out, hist) in enumerate((
                            (vT[:, c, 0:SEQ], uf_p[:, c, w:w + SEQ]),
                            (vT[:, c, SEQ:NT].rearrange("p (s t) -> p s t", t=DEC_T),
                             uf_s[:, c, :, w:w + DEC_T]))):
                        tap = taps[:, c, w:w + 1]
                        if w == 0:
                            V.tensor_scalar(out, hist, tap, vcol("conv_b", c), ALU.mult, ALU.add)\
                                .then_inc(v_ready, 1)
                        else:
                            dve.wait_ge(v_ready, 2 * CT_ * (w - 1) + 2 * c + q + 1)
                            V.scalar_tensor_tensor(out=out, in0=hist, scalar=tap, in1=out,
                                                   op0=ALU.mult, op1=ALU.add).then_inc(v_ready, 1)

            dve.wait_ge(pool_step, 2 + 2 * CT_ + 10)
            dve.wait_ge(st_turned, 4)
            for g, w in enumerate(WINDOWS):
                s_p, s_s = pool_bufs[1 + g % 2]
                early = s_p[:, g, PBUF:PBUF + 16]
                V.tensor_tensor(early, early, icnt[:, g, :], ALU.mult).then_inc(pooled, 1)
                V.scalar_tensor_tensor(out=upT[:, g, 16:SEQ], in0=s_p[:, g, PBUF + 16:PBUF + SEQ],
                                       scalar=1.0 / w, in1=upT[:, g, 16:SEQ],
                                       op0=ALU.mult, op1=ALU.subtract).then_inc(pooled, 1)
                dec = upT[:, g, SEQ:NT].rearrange("p (s t) -> p s t", t=DEC_T)
                V.scalar_tensor_tensor(out=dec, in0=s_s[:, g, :, PBUF:PBUF + DEC_T], scalar=1.0 / w,
                                       in1=dec, op0=ALU.mult, op1=ALU.subtract).then_inc(pooled, 1)
                dve.wait_ge(pooled, 4 * g + 1)
                V.tensor_tensor(upT[:, g, 0:16], early, upT[:, g, 0:16], ALU.subtract).then_inc(pooled, 1)

            dve.wait_ge(v_ready, 2 * CT_ * TAPS)
            dve.wait_ge(mean_done, 1)
            V.tensor_tensor(vT, vT, ps[:, 4, 0:NT].unsqueeze(1).to_broadcast([P, CT_, NT]), ALU.subtract)\
                .then_inc(centred, 1)
            dve.wait_ge(vrms, 1)
            link(V.reciprocal(rstd[:, :], rms[:, :]))
            dve.wait_ge(centred, 1)
            link(V.tensor_tensor(vT, vT, rstd[:, :].unsqueeze(1).to_broadcast([P, CT_, NT]), ALU.mult))
            for c in range(CT_):
                V.tensor_scalar(vT[:, c, :], vT[:, c, :], vcol("conv_ln_g", c), vcol("conv_ln_b", c),
                                ALU.mult, ALU.add).then_inc(ln_ready, 1)
            for c in range(CT_):
                dve.wait_ge(ln_sig, c + 1)
                V.tensor_tensor(vT[:, c, :], vT[:, c, :], gateT[:, c, :], ALU.mult).then_inc(vact, 1)

            dve.wait_ge(z_out, 28)
            for t in range(KT):
                dve.wait_ge(yp_done, t + 1)
                V.scalar_tensor_tensor(out=sgT[:, KT + t, :], in0=ps[:, t % 4, 0:NT],
                                       scalar=vcol("pool_scale", t), in1=sgT[:, KT + t, :],
                                       op0=ALU.mult, op1=ALU.mult).then_inc(yp_out, 1)
            mod_out(1, 7)
            for t in range(KT):
                dve.wait_ge(yc_done, t + 1)
                link(V.tensor_tensor(sgT[:, t, :], ps[:, t % 4, 0:NT], sgT[:, t, :], ALU.mult))
                V.tensor_tensor(hT[:, t, :], sgT[:, t, :], sgT[:, KT + t, :], ALU.add).then_inc(m_ready, 1)
            def residual(t, y, gt, done):
                link(V.tensor_tensor(y[1], y[1], modT[:, gt * KT + t, 1:SEQS].unsqueeze(2)
                                     .to_broadcast([P, DEC_B, DEC_T]), ALU.mult) if y[2] is None else
                     V.tensor_tensor(y[2], y[1], modT[:, gt * KT + t, 1:SEQS].unsqueeze(2)
                                     .to_broadcast([P, DEC_B, DEC_T]), ALU.mult))
                V.scalar_tensor_tensor(out=xT[:, t, 0:SEQ], in0=y[0], scalar=modT[:, gt * KT + t, 0:1],
                                       in1=xT[:, t, 0:SEQ], op0=ALU.mult, op1=ALU.add)
                xs = xT[:, t, SEQ:NT].rearrange("p (s t) -> p s t", t=DEC_T)
                V.tensor_tensor(xs, xs, y[1] if y[2] is None else y[2], ALU.add).then_inc(done, 1)

            for t in range(KT):
                dve.wait_ge(yo_done, t + 1)
                tmp = rstd[:, t * DEC:(t + 1) * DEC].rearrange("p (s t) -> p s t", t=DEC_T)
                residual(t, (ps[:, t % 4, 0:SEQ],
                             ps[:, t % 4, SEQ:NT].rearrange("p (s t) -> p s t", t=DEC_T), tmp), 2, x2_out)
            mod_out(2, 7)
            gain(4, "norm_ffn")
            dve.wait_ge(rms2, 1)
            dve.wait_ge(x2_out, KT)
            modulate(3, 4, h2)

            link(V.memset(lg[:, :, :], 0.0))
            dve.wait_ge(logits, 1)
            dve.wait_ge(ld_late, 48)
            for j, (_, n) in enumerate(TOK_TILES):
                ins = V.tensor_tensor(lg[0:n, j, :], ps[0:n, 5, j * NE:(j + 1) * NE], brout[0:n, :], ALU.add)
            link(ins)
            for j in range(NJ):
                ins = V.max(out=top8[:, j, :], in_=lg[:, j, :])
            link(ins)
            fourth = top8[:, :, TOPK - 1:TOPK].to_broadcast([P, NJ, NE])
            V.tensor_tensor(mask[:, :, :], lg[:, :, :], fourth, ALU.is_gt)
            link(V.tensor_tensor(eq[:, :, :], lg[:, :, :], fourth, ALU.is_equal))
            V.tensor_tensor(lg[:, :, :], lg[:, :, :], top8[:, :, 0:1].to_broadcast([P, NJ, NE]),
                            ALU.subtract).then_inc(shifted, 1)
            V.tensor_reduce(need[:, :], mask[:, :, :], AX.X, ALU.add)
            onesv = ones[:, 0:NE]
            for j in range(NJ):
                ins = V.tensor_tensor_scan(cum[:, j, :], onesv, eq[:, j, :], 0.0, ALU.mult, ALU.add)
            link(ins)
            link(V.tensor_tensor(cum[:, :, :], cum[:, :, :], need[:, :].unsqueeze(2)
                                 .to_broadcast([P, NJ, NE]), ALU.add))
            link(V.scalar_tensor_tensor(out=eq[:, :, :], in0=cum[:, :, :], scalar=float(TOPK) + 0.5,
                                        in1=eq[:, :, :], op0=ALU.is_lt, op1=ALU.mult))
            link(V.tensor_tensor(mask[:, :, :], mask[:, :, :], eq[:, :, :], ALU.add))
            V.memset(mask[DEC:2 * DEC, NJ - 1, :], 0.0)
            V.memset(mask[2 * DEC:P, NJ - 1, :], 0.0).then_inc(mask_ready, 1)
            dve.wait_ge(mask_ready, 1)
            dve.wait_ge(expd, 1)
            link(V.tensor_tensor(wgt[:, :, :], wgt[:, :, :], mask[:, :, :], ALU.mult))
            link(V.tensor_reduce(need[:, :], wgt[:, :, :], AX.X, ALU.add))
            link(V.tensor_scalar(need[:, :], need[:, :], 1e-30, None, ALU.max))
            link(V.reciprocal(need[:, :], need[:, :]))
            V.tensor_tensor(wgt[:, :, :], wgt[:, :, :], need[:, :].unsqueeze(2)
                            .to_broadcast([P, NJ, NE]), ALU.mult).then_inc(wgt_ready, 1)
            dve.wait_ge(ranked, 1)
            rk = ps[:, 6, 0:NJ * NE].rearrange("p (j e) -> p j e", e=NE)
            link(V.scalar_tensor_tensor(out=eq[:, :, :], in0=rk, scalar=1.0, in1=mask[:, :, :],
                                        op0=ALU.add, op1=ALU.mult))
            link(V.tensor_scalar(rankm[:, :, 0:NE], eq[:, :, :], -1.0, None, ALU.add))
            link(V.tensor_copy(cntf[:, 1:NE + 1], ps[0:1, 6, NJ * NE:(NJ + 1) * NE]))
            link(V.tensor_reduce(cntf[:, NE + 2:NE + 3], cntf[:, 1:NE + 1], AX.X, ALU.max))
            V.tensor_copy(cnti[:, :], cntf[:, :]).then_inc(rank_ready, 1)
            counts = ps[:, 6, NJ * NE:(NJ + 1) * NE]
            link(V.tensor_scalar(starts[:, 1, :], counts, NARROW + 0.5, float(NARROW), ALU.is_gt, ALU.mult))
            V.memset(rtab[:, :, :, NE:NE + 1], -1.0)
            V.tensor_copy(rtab[:, 0, :, 0:NE], rankm[:, :, 0:NE])
            for q in range(1, NH):
                ins = V.tensor_tensor(rtab[:, q, :, 0:NE], rankm[:, :, 0:NE],
                                      starts[:, q, :].unsqueeze(1).to_broadcast([P, NJ, NE]), ALU.subtract)
            link(ins)
            dve.wait_ge(wT_turned, 1)
            V.tensor_copy(wT[:, :], ps[0:NE, 5, 0:NT]).then_inc(wT_out, 1)
            dve.wait_ge(wT_out, 1)
            dve.wait_ge(h2_out, 2 * NJ)
            V.memset(ps[:, HG_BANK:T_BANK + 2, :], 0.0).then_inc(turn_clear, 1)
            dve.wait_ge(bd_out, KT)
            V.memset(ps[:, 0:3, :], 0.0).then_inc(added, 1)
            V.memset(yrow, 0.0).then_inc(y_out, 1)

            def hot_for(e):
                for j in range(NJ):
                    ins = V.tensor_scalar(hot[:, j, :], iota[:, :], rankm[:, j, bass.ds(e, 1)], None,
                                          ALU.is_equal)
                ins.then_inc(hot_ready, 1)

            def sel_for(e):
                V.tensor_scalar(sel[:, :], ones[:, :], ident[:, bass.ds(e, 1)], None, ALU.mult)\
                    .then_inc(sel_ready, 1)

            def expert_pass(n0, p):
                dve.wait_ge(pass_ready, p + 1)
                hot_for(0)
                sel_for(0)
                V.memset(comb, 0.0).then_inc(comb_out, 1)
                with dve.Fori(0, NE) as e:
                    n = n0 + e
                    dve.wait_ge(gathered, p * GAT + e + 1)
                    hot_for(e + 1)
                    for j in range(NJ):
                        for q in range(NH):
                            ins = V.tensor_scalar(hotw[:, j, q * NARROW:(q + 1) * NARROW], iota[:, 0:NARROW],
                                                  rtab[:, q, j, bass.ds(e, 1)],
                                                  wgt[:, j, bass.ds(e, 1)], ALU.is_equal, ALU.mult)
                    ins.then_inc(hotw_ready, 1)
                    for h in range(2):
                        dve.wait_ge(chunk_used, NMIX + n * EXPERT_CHUNKS + 2 * h + 1)
                        if h == 1:
                            dve.wait_ge(o_ready, 2 * n + 1)
                        V.tensor_scalar(glu, ps[:, UP_BANKS[2 * h], :], LIMIT, None, ALU.min)\
                            .then_inc(glu_out, 1)
                        dve.wait_ge(chunk_used, NMIX + n * EXPERT_CHUNKS + 2 * h + 2)
                        V.tensor_scalar(otok[:, h, :], ps[:, UP_BANKS[2 * h + 1], :], LIMIT, -LIMIT,
                                        ALU.min, ALU.max).then_inc(lin_clip, 1)
                        if h == 0:
                            add_results(p * GAT + e)
                        dve.wait_ge(sig_out, 2 * n + h + 1)
                        dve.wait_ge(glu_out, 2 * n + h + 1)
                        V.tensor_tensor(glu, glu, sig, ALU.mult)\
                            .then_inc(gs_out, 1)
                        dve.wait_ge(lin_clip, 2 * n + h + 1)
                        dve.wait_ge(gs_out, 2 * n + h + 1)
                        V.scalar_tensor_tensor(out=otok[:, h, :], in0=otok[:, h, :], scalar=1.0,
                                               in1=glu, op0=ALU.add, op1=ALU.mult)\
                            .then_inc(o_ready, 1)
                        if h == 0:
                            dve.wait_ge(comb_turned, n + 1)
                            V.tensor_copy(comb, ps[:, T_BANK + 2, 0:NT]).then_inc(comb_out, 1)
                    sel_for(e + 1)
                add_results(p * GAT + NE)

            def add_results(r):
                for i, k in enumerate(SUM_ORDER):
                    dve.wait_ge(combined, KT * r + i + 1)
                    dve.wait_ge(added, KT * r + 1)
                    V.tensor_tensor(accT[:, k, :], accT[:, k, :], ps[:, T_BANK + i % 3, 0:NT], ALU.add)\
                        .then_inc(added, 1)

            V.memset(need[:, :], 0.0).then_inc(pass_ready, 1)
            expert_pass(0, 0)
            dve.wait_ge(added, KT * GAT + 1)
            most = dve.value_load(cnti[0:1, NE + 2:NE + 3], min_val=0, max_val=NT)
            with dve.If(most > SLOTS):
                with dve.Fori(1, PASSES) as p:
                    dve.wait_ge(hotw_ready, p * NE)
                    dve.wait_ge(hot_ready, p * GAT)
                    V.tensor_scalar(rankm[:, :, :], rankm[:, :, :], float(-SLOTS), None, ALU.add)\
                        .then_inc(rank_ready, 1)
                    dve.wait_ge(rank_ready, p + 1)
                    for q in range(NH):
                        ins = V.tensor_scalar(rtab[:, q, :, :], rankm[:, :, :], float(-q * NARROW), None, ALU.add)
                    ins.then_inc(pass_ready, 1)
                    expert_pass(p * NE, p)
                    dve.wait_ge(added, (p + 1) * (KT * GAT) + 1)

            for t in range(KT):
                residual(t, (accT[:, t, 0:SEQ],
                             accT[:, t, SEQ:NT].rearrange("p (s t) -> p s t", t=DEC_T), None), 5, x3_out)
            dve.wait_ge(rms3, 1)
            link(V.reciprocal(rstd[:, :], rms[:, :]))
            dve.wait_ge(x3_out, KT)
            for t in range(KT):
                V.scalar_tensor_tensor(out=hT[:, t, :], in0=xT[:, t, :], scalar=vcol("norm_final", t),
                                       in1=rstd[:, :], op0=ALU.mult, op1=ALU.mult).then_inc(yn, 1)

        @block.tensor
        def _(pe):
            def chunk(c, k):
                return ring[:, c % RING, :].rearrange("p (k n) -> p k n", k=k)

            def chunk_landed(c):
                pe.wait_ge(landed[c % RING], 16 * (c // RING + 1))

            pe.wait_ge(consts, 6)
            for g in range(16):
                bank = ps[:, g % 8, :]
                if g >= 8:
                    pe.wait_ge(turn_out, g - 7)
                if g == 0:
                    pe.wait_ge(ld_vec, 16 * len(VEC_ROWS))
                    ins = pe.transpose(bank[:, 0:NVEC], vec_rows[0:NVEC, :], ident[0:NVEC, 0:NVEC])
                elif g < 9:
                    pe.wait_ge(ld_x, 32)
                    for j, (t0, n) in enumerate(TOK_TILES):
                        ins = pe.transpose(bank[:, t0:t0 + n], rows[0:n, j, (g - 1) * P:g * P],
                                           ident[0:n, 0:n])
                elif g == 9:
                    pe.wait_ge(silu_c, 2)
                    for k in range(KT):
                        ins = pe.transpose(bank[:, k * SEQS:(k + 1) * SEQS], c_rows[:, k * P:(k + 1) * P],
                                           ident[0:SEQS, 0:SEQS])
                elif g == 10:
                    pe.wait_ge(ld_taps, 16)
                    for c in range(CT_):
                        ins = pe.transpose(bank[:, c * TAPS:(c + 1) * TAPS], tap_rows[:, c * P:(c + 1) * P],
                                           ident[0:TAPS, 0:TAPS])
                elif g < 15:
                    pe.wait_ge(ld_state, 32)
                    for j in range(2):
                        ins = pe.transpose(bank[:, j * 120:(j + 1) * 120],
                                           sconv_rows[:, j, (g - 11) * P:(g - 10) * P], ident[0:120, 0:120])
                else:
                    for c in range(CT_):
                        ins = pe.transpose(bank[:, c * 120:(c + 1) * 120], spool_rows[:, c * P:(c + 1) * P],
                                           ident[0:120, 0:120])
                ins.then_inc(turned, 1)

            def channel_sums(bank, src, weight, tiles, ready, done):
                for k in range(tiles):
                    if ready is not None:
                        pe.wait_ge(ready, k + 1)
                    ins = pe.matmul(ps[:, bank, 0:NT], avg[:, weight, :], src[:, k, :],
                                    start=(k == 0), stop=(k == tiles - 1))
                ins.then_inc(done, 1)

            def modulation(g, bank):
                for q in range(MOD_CHUNKS):
                    c = MIX_AT["ada", MOD_CHUNKS * g + q]
                    w = chunk(c, KT)
                    chunk_landed(c)
                    for k in range(KT):
                        for a in range(4):
                            ins = pe.matmul(ps[a * CW:(a + 1) * CW, bank, q * P:(q + 1) * P], silc[:, k, :],
                                            w[:, k, a * P:(a + 1) * P], start=(k == 0), stop=(k == KT - 1))
                    ins.then_inc(chunk_used, 1)

            def turn_modulation(g, bank):
                pe.wait_ge(mod_rows, g + 1)
                for q in range(MOD_CHUNKS):
                    ins = pe.transpose(ps[:, bank, q * P:(q + 1) * P], mod_rows_of[g][:, q * P:(q + 1) * P],
                                       ident[:, :])
                ins.then_inc(mod_turned, 1)

            pe.wait_ge(turn_out, 12)
            channel_sums(1, sq, 0, KT, sq1, stat1)
            modulation(0, 2)
            turn_modulation(0, 3)

            pe.wait_ge(h1, KT)
            for i in range(7):
                c = MIX_AT["in", i]
                w = chunk(c, KT)
                chunk_landed(c)
                for m in range(4):
                    t = 4 * i + m
                    if t >= 8:
                        pe.wait_ge(z_out, t - 7)
                    for k in range(KT):
                        ins = pe.matmul(ps[:, t % 8, 0:NT], w[:, k, m * P:(m + 1) * P], hT[:, k, :],
                                        start=(k == 0), stop=(k == KT - 1))
                    ins.then_inc(z_done, 1)
                pe.wait_ge(z_done, 4 * i + 4)
                pe.sem_inc(chunk_used, 1)

            pe.wait_ge(u_ready, CT_)
            for i, (src, t0, t1) in enumerate(((uT, SEQ - CBUF, SEQ), (uT, SEQ, NT),
                                               (upT, SEQ - PBUF, SEQ), (upT, SEQ, NT))):
                pe.wait_ge(z_out, 25 + i)
                for c in range(CT_):
                    ins = pe.transpose(ps[0:t1 - t0, i, c * P:(c + 1) * P], src[:, c, t0:t1], ident[:, :])
                ins.then_inc(st_turned, 1)

            pe.wait_ge(v_ready, 2 * CT_ * TAPS)
            channel_sums(4, vT, 1, CT_, None, mean_done)
            modulation(1, 6)
            pe.wait_ge(vsq, 1)
            channel_sums(5, gateT, 1, CT_, None, var_done)
            turn_modulation(1, 7)

            pe.wait_ge(ld_late, 48)
            pe.wait_ge(pooled, 4 * CT_)
            for t in range(KT):
                if t < 4:
                    pe.wait_ge(st_out, t + 1)
                else:
                    pe.wait_ge(yp_out, t - 3)
                pe.matmul(ps[:, t % 4, 0:NT], wpool[:, t // 2, (t % 2) * P:(t % 2 + 1) * P], upT[:, t // 2, :],
                          start=True, stop=True).then_inc(yp_done, 1)

            c = MIX_AT["conv_out", 0]
            w = chunk(c, CT_)
            chunk_landed(c)
            pe.wait_ge(vact, CT_)
            for t in range(KT):
                if t < 4:
                    pe.wait_ge(yp_out, t + 5)
                else:
                    pe.wait_ge(m_ready, t - 3)
                for k in range(CT_):
                    ins = pe.matmul(ps[:, t % 4, 0:NT], w[:, k, t * P:(t + 1) * P], vT[:, k, :],
                                    start=(k == 0), stop=(k == CT_ - 1))
                ins.then_inc(yc_done, 1)
            pe.wait_ge(yc_done, KT)
            pe.sem_inc(chunk_used, 1)

            pe.wait_ge(m_ready, KT)
            for i in range(2):
                c = MIX_AT["out", i]
                w = chunk(c, KT)
                chunk_landed(c)
                for m in range(4):
                    t = 4 * i + m
                    if t >= 4:
                        pe.wait_ge(x2_out, t - 3)
                    for k in range(KT):
                        ins = pe.matmul(ps[:, t % 4, 0:NT], w[:, k, m * P:(m + 1) * P], hT[:, k, :],
                                        start=(k == 0), stop=(k == KT - 1))
                    ins.then_inc(yo_done, 1)
                pe.wait_ge(yo_done, 4 * i + 4)
                pe.sem_inc(chunk_used, 1)
            modulation(2, 6)
            channel_sums(4, sq, 0, KT, sq2, stat2)
            turn_modulation(2, 7)

            pe.wait_ge(h2, KT)
            for j, (t0, n) in enumerate(TOK_TILES):
                for k in range(KT):
                    ins = pe.matmul(ps[0:n, 5, j * NE:(j + 1) * NE], hT[:, k, t0:t0 + n], wrouter[:, k, :],
                                    start=(k == 0), stop=(k == KT - 1))
            ins.then_inc(logits, 1)
            for j, (t0, n) in enumerate(TOK_TILES):
                for half in range(2):
                    i = 2 * j + half
                    for q in range(4):
                        k = 4 * half + q
                        ins = pe.transpose(ps[0:n, (0, 1, 2, 3, 4, 7)[i], q * P:(q + 1) * P],
                                           hT[:, k, t0:t0 + n], ident[:, :])
                    ins.then_inc(h2_turned, 1)
            pe.wait_ge(mask_ready, 1)
            for j in range(NJ):
                for i in range(j + 1):
                    pe.matmul(ps[:, 6, j * NE:(j + 1) * NE], upper[:, :] if i == j else ones[:, :],
                              mask[:, i, :], start=(i == 0), stop=(i == j))
            for i in range(NJ):
                ins = pe.matmul(ps[:, 6, NJ * NE:(NJ + 1) * NE], ones[:, :], mask[:, i, :],
                                start=(i == 0), stop=(i == NJ - 1))
            ins.then_inc(ranked, 1)
            pe.wait_ge(wgt_ready, 1)
            for j, (t0, n) in enumerate(TOK_TILES):
                ins = pe.transpose(ps[0:NE, 5, t0:t0 + n], wgt[0:n, j, :], ident[0:n, 0:n])
            ins.then_inc(wT_turned, 1)
            pe.wait_ge(wT_out, 1)
            pe.wait_ge(h2_out, 6)
            pe.wait_ge(ld_bdown, 16)
            for t in range(KT):
                if t >= 4:
                    pe.wait_ge(bd_out, t - 3)
                pe.matmul(ps[:, BD_BANKS[t % 4], 0:NT], bdown[:, t * P:(t + 1) * P], wT[:, :],
                          start=True, stop=True).then_inc(bd_done, 1)

            def by_width(count, emit):
                with pe.If(count > NARROW):
                    emit(SLOTS)
                with pe.Else():
                    emit(NARROW)

            def gather(width):
                tiles = SLOTS // width
                cols = COLS // tiles
                for h in range(2):
                    for j, (_, n) in enumerate(TOK_TILES):
                        for a in range(tiles):
                            at = h * COLS + a * cols
                            ins = pe.matmul(ps[a * width:(a + 1) * width, HG_BANK + h, 0:cols],
                                            hot[0:n, j, 0:width], rows[0:n, j, at:at + cols],
                                            start=(j == 0), stop=(j == NJ - 1))
                ins.then_inc(gathered, 1)

            def turn_gathered(g, width):
                for h in range(2):
                    pe.wait_ge(grow_out, 2 * g + h + 1)
                    for b in range(4 * width // SLOTS):
                        ins = pe.transpose(ps[:, HG_BANK + h, b * P:(b + 1) * P],
                                           yrow[:, h * BANK + b * P:h * BANK + (b + 1) * P], ident[:, :])
                    ins.then_inc(g_turned, 1)

            def tile_of(m, width):
                blocks = 4 * width // SLOTS
                return m // blocks, m % blocks

            def products(u, j, width, tokens, bias_at=None):
                slot = EXPERT_RING[(u * EXPERT_CHUNKS + j) % NRING]
                w = slots[slot].rearrange("p (k n) -> p k n", k=KT)
                tiles = SLOTS // width
                cols = COLS // tiles
                for k in range(KT):
                    for a in range(tiles):
                        ins = pe.matmul(ps[a * width:(a + 1) * width, UP_BANKS[j], 0:cols], tokens(k),
                                        w[:, k, a * cols:(a + 1) * cols],
                                        start=(k == 0), stop=(k == KT - 1 and bias_at is None))
                if bias_at is not None:
                    for a in range(tiles):
                        at = bias_at + a * cols
                        ins = pe.matmul(ps[a * width:(a + 1) * width, UP_BANKS[j], 0:cols],
                                        sel[:, 0:width], bup[:, at:at + cols], start=False, stop=True)
                ins.then_inc(chunk_used, 1)

            def expert_chunk_landed(turn, u, j):
                i = u * EXPERT_CHUNKS + j
                slot = EXPERT_RING[i % NRING]
                pe.wait_ge(landed[slot], turn * 16 + 16 * (MIXER_USES[slot] + i // NRING + 1))

            def turned_tokens(xT_, width):
                def tokens(k):
                    a, b = tile_of(k % 4, width)
                    return xT_[:, k // 4, b * P + a * width:b * P + (a + 1) * width]
                return tokens

            def up(n, turn, u, h, width):
                for j in (2 * h, 2 * h + 1):
                    expert_chunk_landed(turn, u, j)
                    if j == 3:
                        pe.wait_ge(glu_out, 2 * n + 1)
                    products(u, j, width, turned_tokens(hgT, width), (0, D, COLS, D + COLS)[j])

            def turn_o(n, r, width):
                pe.wait_ge(added, KT * r + 9)
                for h in range(2):
                    pe.wait_ge(o_ready, 2 * n + h + 1)
                    for b in range(4 * width // SLOTS):
                        ins = pe.transpose(ps[:, T_BANK + h, b * P:(b + 1) * P],
                                           otok[:, h, b * P:(b + 1) * P], ident[:, :])
                    ins.then_inc(o_turned, 1)

            def down(n, turn, u, width):
                pe.wait_ge(oT_out, 2 * n + 2)
                for j in (4, 5):
                    expert_chunk_landed(turn, u, j)
                    products(u, j, width, turned_tokens(oT, width))

            def combine(r, c, width):
                pe.wait_ge(comb_out, c)
                for i, k in enumerate(SUM_ORDER):
                    if i >= 3:
                        pe.wait_ge(added, KT * r + i - 1)
                    a, b = tile_of(k % 4, width)
                    at = (k // 4) * BANK + b * P
                    part = slice(a * width, (a + 1) * width)
                    pe.matmul(ps[:, T_BANK + i % 3, 0:NT], yrow[part, at:at + P], comb[part, :],
                              start=True, stop=True).then_inc(combined, 1)

            def expert_pass(n0, p, fixed):
                def sized(count, emit):
                    if fixed:
                        emit(SLOTS)
                    else:
                        by_width(count, emit)

                pe.wait_ge(hot_ready, p * GAT + 1)
                first = None if fixed else pe.value_load(cnti[0:1, 1:2], min_val=0, max_val=NT)
                sized(first, lambda width: (gather(width), turn_gathered(p * GAT, width)))
                with pe.Fori(0, NE // UNROLL) as step:
                    turn = p * (NE * EXPERT_CHUNKS // NRING) + step * TURNS
                    for u in range(UNROLL):
                        e = step * UNROLL + u
                        n = n0 + e
                        g = p * GAT + e
                        last = this = nxt = None
                        if not fixed:
                            last, this, nxt = (pe.value_load(cnti[0:1, bass.ds(e + i, 1)],
                                                             min_val=0, max_val=NT) for i in range(3))
                        pe.wait_ge(hg_out, 2 * g + 2)
                        pe.wait_ge(sel_ready, g + 1)
                        pe.wait_ge(y_out, 2 * n + 1)
                        sized(this, lambda width: up(n, turn, u, 0, width))
                        sized(last, lambda width: combine(g, g + 1, width))
                        pe.wait_ge(hotw_ready, n + 1)
                        pe.wait_ge(added, KT * g + 7)
                        for j, (t0, nt) in enumerate(TOK_TILES):
                            ins = pe.transpose(ps[:, T_BANK + 2, t0:t0 + nt], hotw[0:nt, j, :],
                                               ident[0:nt, 0:nt])
                        ins.then_inc(comb_turned, 1)
                        sized(this, lambda width: up(n, turn, u, 1, width))
                        pe.wait_ge(hot_ready, g + 2)
                        sized(nxt, gather)
                        sized(this, lambda width: turn_o(n, g, width))
                        sized(nxt, lambda width: turn_gathered(g + 1, width))
                        sized(this, lambda width: down(n, turn, u, width))
                pe.wait_ge(y_out, 2 * n0 + 2 * NE + 1)
                last = None if fixed else pe.value_load(cnti[0:1, NE:NE + 1], min_val=0, max_val=NT)
                sized(last, lambda width: combine(p * GAT + NE, p * GAT + NE + 1, width))

            pe.wait_ge(ld_bup, 16)
            pe.wait_ge(turn_clear, 1)
            pe.wait_ge(y_out, 1)
            pe.wait_ge(added, 1)
            expert_pass(0, 0, False)
            most = pe.value_load(cnti[0:1, NE + 2:NE + 3], min_val=0, max_val=NT)
            with pe.If(most > SLOTS):
                with pe.Fori(1, PASSES) as p:
                    expert_pass(p * NE, p, True)

            channel_sums(0, sq, 0, KT, sq3, stat3)
            pe.wait_ge(yn, KT)
            for j, (t0, n) in enumerate(TOK_TILES):
                for half in range(2):
                    for q in range(4):
                        ins = pe.transpose(ps[0:n, 1 + 2 * j + half, q * P:(q + 1) * P],
                                           hT[:, 4 * half + q, t0:t0 + n], ident[:, :])
                    ins.then_inc(fin_turned, 1)


_INS = ['x_prompt', 'x_sample', 'state_conv', 'state_pool', 'c_prompt', 'c_sample', 'w_ada', 'b_ada',
        'norm_mix', 'w_in', 'b_in', 'conv_w', 'conv_b', 'conv_ln_g', 'conv_ln_b', 'w_conv_out', 'w_pool',
        'pool_scale', 'w_out', 'norm_ffn', 'w_router', 'b_router', 'w_up', 'b_up', 'w_down', 'b_down',
        'norm_final']
_OUTS = [(1, SEQ, D), (DEC_B, DEC_T, D), (1, 1, CBUF, DC), (1, 1, PBUF, DC),
         (1, DEC_B, CBUF, DC), (1, DEC_B, PBUF, DC)]


def kernel(**inputs):
    import numpy as np
    import concourse.bacc as bacc
    from concourse.bass_utils import run_bass_kernel_spmd

    nc = bacc.Bacc("TRN2", target_bir_lowering=False, num_devices=1)
    arrays, args = {}, []
    for name in _INS:
        a = np.ascontiguousarray(inputs[name])
        arrays[f"in_{name}_dram"] = a
        args.append(nc.dram_tensor(f"in_{name}_dram", a.shape, mybir.dt.from_np(a.dtype),
                                   kind="ExternalInput").ap())
    for i, shape in enumerate(_OUTS):
        args.append(nc.dram_tensor(f"out_{i}_dram", shape, F32, kind="ExternalOutput").ap())
    build(nc, *args)
    r = run_bass_kernel_spmd(nc, [arrays], core_ids=[0])
    return tuple(r.results[0][f"out_{i}_dram"] for i in range(len(_OUTS)))
```
